# Optimizing a Trainium2 kernel written in Bass

```python
import math
import jax, jax.numpy as jnp
from jax import lax
import numpy as np

D_MODEL = 1024
BATCH = 1
SEQ = 2048
DEPTH = 1
DEC_BATCH = 8
DEC_SEQ = 8
PAST_LEN = 2048
PAGE_SIZE = 128

HEAD_DIM = 64
MIX_WIDTH = D_MODEL
A_WIDTH = 3 * MIX_WIDTH // 8
A_HEADS = A_WIDTH // HEAD_DIM
B_WIDTH = 3 * MIX_WIDTH // 8
B_HEADS = B_WIDTH // HEAD_DIM
B_KV_HEADS = B_HEADS // 3
B_KV_WIDTH = B_KV_HEADS * HEAD_DIM
C_WIDTH = MIX_WIDTH - A_WIDTH - B_WIDTH
A_PATTERNS = ((128, 1), (512, 4), (2048, 16))
A_MAX_WINDOW = 2048
B_WINDOW = 128
CONV_WIDTH = 3
FF_DIM = 4 * D_MODEL
NUM_BUCKETS = 32
MAX_DISTANCE = 2048
BLOCK = 128
EPS = 1e-6
SCALE = 1.0 / math.sqrt(HEAD_DIM)
_IN_SIZES = (A_WIDTH, A_WIDTH, A_WIDTH, B_WIDTH, B_KV_WIDTH, B_KV_WIDTH, C_WIDTH, C_WIDTH, C_WIDTH)
IN_WIDTH = sum(_IN_SIZES)
IN_SPLITS = tuple(int(s) for s in np.cumsum(_IN_SIZES)[:-1])

kernel_name = 'hybrid_dilated_swa_conv_decoder_step'

def rmsnorm(x, g):
    xf = x.astype(jnp.float32)
    y = xf * lax.rsqrt(jnp.mean(xf * xf, axis=-1, keepdims=True) + EPS)
    return (y * g.astype(jnp.float32)).astype(x.dtype)

def t5_bucket(dist):
    dist = jnp.maximum(dist, 0)
    max_exact = NUM_BUCKETS // 2
    scaled = jnp.log(jnp.maximum(dist, 1).astype(jnp.float32) / max_exact) / math.log(MAX_DISTANCE / max_exact)
    large = max_exact + (scaled * (NUM_BUCKETS - max_exact)).astype(jnp.int32)
    large = jnp.minimum(large, NUM_BUCKETS - 1)
    return jnp.where(dist < max_exact, dist, large)

def strided_band_attention(q, k, v, table, d, wk):
    n_b, s_len, n_h, hd = q.shape
    n_kv = k.shape[2]
    g = n_h // n_kv
    span = d * BLOCK
    s_pad = -(-s_len // span) * span
    sub = s_pad // d
    nb = sub // BLOCK

    def to_sub(t):
        t = jnp.pad(t, ((0, 0), (0, s_pad - s_len), (0, 0), (0, 0)))
        t = t.reshape(n_b, sub, d, t.shape[2], hd).transpose(0, 2, 1, 3, 4)
        return t.reshape(n_b * d, nb, BLOCK, t.shape[3], hd)

    def prev(t):
        return jnp.pad(t, ((0, 0), (1, 0), (0, 0), (0, 0), (0, 0)))[:, :-1]

    qb = to_sub(q).reshape(n_b * d, nb, BLOCK, n_kv, g, hd)
    kb = to_sub(k)
    vb = to_sub(v)
    kk = jnp.concatenate([prev(kb), kb], axis=2)
    vv = jnp.concatenate([prev(vb), vb], axis=2)
    qi = jnp.arange(BLOCK)[:, None]
    kj = jnp.arange(2 * BLOCK)[None, :]
    delta = BLOCK + qi - kj
    in_band = (delta >= 0) & (delta <= wk)
    bias = table[t5_bucket(delta * d)].astype(jnp.float32)
    bias = bias.reshape(BLOCK, 2 * BLOCK, n_kv, g).transpose(2, 3, 0, 1)
    has_prev = (jnp.arange(nb)[:, None, None] > 0) | (kj[None] >= BLOCK)
    mask = in_band[None] & has_prev
    s = jnp.einsum('nbqkgd,nbjkd->nbkgqj', qb, kk, preferred_element_type=jnp.float32) * SCALE + bias
    s = jnp.where(mask[None, :, None, None], s, -jnp.inf)
    m = jnp.max(s, axis=-1, keepdims=True)
    p = jnp.exp(s - m)
    l = jnp.sum(p, axis=-1, keepdims=True)
    o = jnp.einsum('nbkgqj,nbjkd->nbqkgd', p / l, vv.astype(jnp.float32))
    lse = (m + jnp.log(l))[..., 0]
    o = o.reshape(n_b, d, sub, n_h, hd).transpose(0, 2, 1, 3, 4).reshape(n_b, s_pad, n_h, hd)[:, :s_len]
    lse = lse.transpose(0, 1, 4, 2, 3).reshape(n_b, d, sub, n_h).transpose(0, 2, 1, 3)
    lse = lse.reshape(n_b, s_pad, n_h)[:, :s_len]
    return o, lse

def gather_attention(q, k_cat, v_cat, table, d, wk, buf_len):
    n_b, t_len, n_h, hd = q.shape
    n_kv = k_cat.shape[2]
    g = n_h // n_kv
    j = jnp.arange(wk + 1)
    idx = buf_len + jnp.arange(t_len)[:, None] - j[None, :] * d
    valid = idx >= 0
    idx = jnp.maximum(idx, 0)
    kg = jnp.take(k_cat, idx, axis=1)
    vg = jnp.take(v_cat, idx, axis=1)
    bias = table[t5_bucket(j * d)].astype(jnp.float32).reshape(wk + 1, n_kv, g).transpose(1, 2, 0)
    qg = q.reshape(n_b, t_len, n_kv, g, hd)
    s = jnp.einsum('btkgd,btjkd->btkgj', qg, kg, preferred_element_type=jnp.float32) * SCALE + bias
    s = jnp.where(valid[None, :, None, None, :], s, -jnp.inf)
    m = jnp.max(s, axis=-1, keepdims=True)
    p = jnp.exp(s - m)
    l = jnp.sum(p, axis=-1, keepdims=True)
    o = jnp.einsum('btkgj,btjkd->btkgd', p / l, vg.astype(jnp.float32)).reshape(n_b, t_len, n_h, hd)
    lse = (m + jnp.log(l))[..., 0].reshape(n_b, t_len, n_h)
    return o, lse

def combine_by_denominator(outs, lses):
    wts = jax.nn.softmax(jnp.stack(lses, axis=0), axis=0)
    return jnp.sum(wts[..., None] * jnp.stack(outs, axis=0), axis=0)

def project(h, w_in_l):
    n_b, t_len = h.shape[:2]
    proj = jnp.einsum('btd,de->bte', h, w_in_l)
    aq, ak, av, bq, bk, bv, cb, cc, cx = jnp.split(proj, IN_SPLITS, axis=-1)

    def heads(t, n):
        return t.reshape(n_b, t_len, n, HEAD_DIM)

    return (heads(aq, A_HEADS), heads(ak, A_HEADS), heads(av, A_HEADS),
            heads(bq, B_HEADS), heads(bk, B_KV_HEADS), heads(bv, B_KV_HEADS), cb, cc * cx)

def causal_conv(u_ext, w, t_len):
    return sum(w[i] * u_ext[:, i:i + t_len] for i in range(CONV_WIDTH))

def merge_out(o_a, o_b, o_c, w_out_l, dtype):
    n_b, t_len = o_c.shape[:2]
    mix = jnp.concatenate([o_a.reshape(n_b, t_len, A_WIDTH).astype(dtype),
                           o_b.reshape(n_b, t_len, B_WIDTH).astype(dtype),
                           o_c.astype(dtype)], axis=-1)
    return jnp.einsum('btm,md->btd', mix, w_out_l)

def mixer_prompt(h, w_in_l, w_out_l, conv_w_l, sink_l, rel_bias):
    aq, ak, av, bq, bk, bv, cb, u = project(h, w_in_l)
    t_len = h.shape[1]
    outs, lses = [], []
    for w, d in A_PATTERNS:
        o, lse = strided_band_attention(aq, ak, av, rel_bias[:, :A_HEADS], d, w // d)
        outs.append(o)
        lses.append(lse)
    o_a = combine_by_denominator(outs, lses)
    o_b, lse_b = strided_band_attention(bq, bk, bv, rel_bias[:, A_HEADS:], 1, B_WINDOW)
    o_b = o_b * jax.nn.sigmoid(lse_b - sink_l.astype(jnp.float32))[..., None]
    u_ext = jnp.pad(u, ((0, 0), (CONV_WIDTH - 1, 0), (0, 0)))
    o_c = cb * causal_conv(u_ext, conv_w_l, t_len)
    out = merge_out(o_a, o_b, o_c, w_out_l, h.dtype)
    new = (ak[:, -A_MAX_WINDOW:], av[:, -A_MAX_WINDOW:], bk[:, -B_WINDOW:], bv[:, -B_WINDOW:],
           u[:, -(CONV_WIDTH - 1):])
    return out, new

def mixer_sample(h, ck_a, cv_a, ck_b, cv_b, conv_state, w_in_l, w_out_l, conv_w_l, sink_l, rel_bias):
    aq, ak, av, bq, bk, bv, cb, u = project(h, w_in_l)
    t_len = h.shape[1]
    buf_a = ck_a.shape[1]
    buf_b = ck_b.shape[1]
    ka = jnp.concatenate([ck_a.astype(ak.dtype), ak], axis=1)
    va = jnp.concatenate([cv_a.astype(av.dtype), av], axis=1)
    kb = jnp.concatenate([ck_b.astype(bk.dtype), bk], axis=1)
    vb = jnp.concatenate([cv_b.astype(bv.dtype), bv], axis=1)
    outs, lses = [], []
    for w, d in A_PATTERNS:
        o, lse = gather_attention(aq, ka, va, rel_bias[:, :A_HEADS], d, w // d, buf_a)
        outs.append(o)
        lses.append(lse)
    o_a = combine_by_denominator(outs, lses)
    o_b, lse_b = gather_attention(bq, kb, vb, rel_bias[:, A_HEADS:], 1, B_WINDOW, buf_b)
    o_b = o_b * jax.nn.sigmoid(lse_b - sink_l.astype(jnp.float32))[..., None]
    u_ext = jnp.concatenate([conv_state.astype(u.dtype), u], axis=1)
    o_c = cb * causal_conv(u_ext, conv_w_l, t_len)
    out = merge_out(o_a, o_b, o_c, w_out_l, h.dtype)
    new = (ka[:, -A_MAX_WINDOW:], va[:, -A_MAX_WINDOW:], kb[:, -B_WINDOW:], vb[:, -B_WINDOW:],
           u_ext[:, -(CONV_WIDTH - 1):])
    return out, new

def ffn_sublayer(x, g_pre, w_up_l, w_down_l, g_post):
    h = rmsnorm(x, g_pre)
    a = jax.nn.relu(jnp.einsum('btd,df->btf', h, w_up_l))
    return x + rmsnorm(jnp.einsum('btf,fd->btd', a * a, w_down_l), g_post)

def setup_inputs(seed: int = 0) -> dict:
    key = jax.random.key(seed)
    ks = jax.random.split(key, 20)
    f32 = jnp.float32
    buf_a = min(A_MAX_WINDOW, PAST_LEN)
    buf_b = min(B_WINDOW, PAST_LEN)

    def nrm(k, shape, s=1.0):
        return s * jax.random.normal(k, shape, f32)

    return {
        'x_prompt': nrm(ks[0], (BATCH, SEQ, D_MODEL)),
        'x_sample': nrm(ks[1], (DEC_BATCH, DEC_SEQ, D_MODEL)),
        'cache_a_k': nrm(ks[2], (DEPTH, DEC_BATCH, buf_a, A_HEADS, HEAD_DIM)),
        'cache_a_v': nrm(ks[3], (DEPTH, DEC_BATCH, buf_a, A_HEADS, HEAD_DIM)),
        'cache_b_k': nrm(ks[4], (DEPTH, DEC_BATCH, buf_b, B_KV_HEADS, HEAD_DIM)),
        'cache_b_v': nrm(ks[5], (DEPTH, DEC_BATCH, buf_b, B_KV_HEADS, HEAD_DIM)),
        'state_conv': nrm(ks[6], (DEPTH, DEC_BATCH, CONV_WIDTH - 1, C_WIDTH)),
        'w_in': nrm(ks[7], (DEPTH, D_MODEL, IN_WIDTH), D_MODEL ** -0.5),
        'w_out': nrm(ks[8], (DEPTH, MIX_WIDTH, D_MODEL), MIX_WIDTH ** -0.5),
        'conv_w': nrm(ks[9], (DEPTH, CONV_WIDTH, C_WIDTH), 0.5),
        'b_sinks': nrm(ks[10], (DEPTH, B_HEADS)),
        'rel_bias': nrm(ks[11], (NUM_BUCKETS, A_HEADS + B_HEADS), 0.5),
        'g_mix_pre': 1.0 + nrm(ks[12], (DEPTH, D_MODEL), 0.1),
        'g_mix_post': 1.0 + nrm(ks[13], (DEPTH, D_MODEL), 0.1),
        'w_up': nrm(ks[14], (DEPTH, D_MODEL, FF_DIM), D_MODEL ** -0.5),
        'w_down': nrm(ks[15], (DEPTH, FF_DIM, D_MODEL), FF_DIM ** -0.5),
        'g_mlp_pre': 1.0 + nrm(ks[16], (DEPTH, D_MODEL), 0.1),
        'g_mlp_post': 1.0 + nrm(ks[17], (DEPTH, D_MODEL), 0.1),
    }

def reference(x_prompt, x_sample, cache_a_k, cache_a_v, cache_b_k, cache_b_v, state_conv,
              w_in, w_out, conv_w, b_sinks, rel_bias, g_mix_pre, g_mix_post, w_up, w_down,
              g_mlp_pre, g_mlp_post):
    xp = x_prompt
    xs = x_sample
    new_p = [[], [], [], [], []]
    new_s = [[], [], [], [], []]
    for l in range(DEPTH):
        mp, st_p = mixer_prompt(rmsnorm(xp, g_mix_pre[l]), w_in[l], w_out[l], conv_w[l], b_sinks[l], rel_bias)
        xp = xp + rmsnorm(mp, g_mix_post[l])
        xp = ffn_sublayer(xp, g_mlp_pre[l], w_up[l], w_down[l], g_mlp_post[l])
        ms, st_s = mixer_sample(rmsnorm(xs, g_mix_pre[l]), cache_a_k[l], cache_a_v[l], cache_b_k[l],
                                cache_b_v[l], state_conv[l], w_in[l], w_out[l], conv_w[l], b_sinks[l],
                                rel_bias)
        xs = xs + rmsnorm(ms, g_mix_post[l])
        xs = ffn_sublayer(xs, g_mlp_pre[l], w_up[l], w_down[l], g_mlp_post[l])
        for i in range(5):
            new_p[i].append(st_p[i])
            new_s[i].append(st_s[i])
    a_k_p, a_v_p, b_k_p, b_v_p, conv_p = [jnp.stack(t, axis=0) for t in new_p]
    a_k_s, a_v_s, b_k_s, b_v_s, conv_s = [jnp.stack(t, axis=0) for t in new_s]
    return (xp, xs, a_k_p, a_v_p, b_k_p, b_v_p, conv_p, a_k_s, a_v_s, b_k_s, b_v_s, conv_s)


_drawn_inputs = setup_inputs


def setup_inputs(seed=0):
    import zlib

    import numpy as np

    out = dict(_drawn_inputs(seed))
    spreads = {}
    factors = {}
    for name, (base, spread) in spreads.items():
        noise = np.random.default_rng([zlib.crc32(name.encode()), seed]).standard_normal(out[name].shape)
        drawn = base * np.exp(spread * noise) if base else spread * noise
        out[name] = __import__('jax').numpy.asarray(drawn.astype(out[name].dtype))
    for name, factor in factors.items():
        out[name] = (out[name] * factor).astype(out[name].dtype)
    return out
```

```python
from contextlib import ExitStack
import math

import numpy as np
import concourse.bass as bass
from concourse import mybir

F32 = mybir.dt.float32
F32R = mybir.dt.float32r
ALU = mybir.AluOpType
ACT = mybir.ActivationFunctionType
AX = mybir.AxisListType.X

P = 128
D = 1024
SEQ = 2048
DEC_B, DEC_T = 8, 8
DEC = DEC_B * DEC_T
TOK = SEQ + DEC
TILES = SEQ // P
HD = 64
AH, BH, KVH = 6, 6, 2
AW = AH * HD
BW = BH * HD
KVW = KVH * HD
CW = D - AW - BW
PAST = 2048
BWIN = 128
IN_W = 3 * AW + BW + 2 * KVW + 3 * CW
FBLK = IN_W // P
DBLK = D // P
FF = 4 * D
EPS = 1e-6
SCALE = HD ** -0.5
MASKED = -1e30
BUCKETS = 32
AQ0, AK0, AV0, BQ0, BK0, BV0, CB0, CC0, CX0 = 0, 3, 6, 9, 12, 13, 14, 16, 18
GRP = 352
NGRP = TOK // GRP
assert NGRP * GRP == TOK


def apart(engine):
    engine.nop(nofuse=True)


def f32(ap):
    return ap.bitcast(F32)


class Phase:

    def __init__(self, nc, name):
        self.nc, self.name, self.ctx, self.semaphores = nc, name, ExitStack(), []

    def __enter__(self):
        return self

    def __exit__(self, *exc):
        self.ctx.__exit__(*exc)
        self.nc.clear_and_free_semaphores(self.semaphores)
        self.nc.all_engine_barrier()

    def sb(self, name, shape, dt=F32):
        return self.ctx.enter_context(self.nc.sbuf_tensor(f"{self.name}_{name}", shape, dt))

    def banks(self, name, n):
        return [self.ctx.enter_context(self.nc.psum_tensor(f"{self.name}_{name}{i}", [P, 512], F32)) for i in range(n)]

    def sem(self, name):
        self.semaphores.append(self.nc.alloc_semaphore(f"{self.name}_{name}"))
        return self.semaphores[-1]

    def sems(self, name, n):
        return [self.sem(f"{name}{i}") for i in range(n)]

    def block(self):
        return self.ctx.enter_context(self.nc.Block())


def copy_cache(engine, cache, out, b, pieces, done):
    rows, width = cache.shape[2], cache.shape[3] * cache.shape[4]
    cache, out = (a.rearrange("l b t h e -> (l b) (t h e)") for a in (cache, out))
    frm = cache[:, DEC_T * width:].rearrange("b (x n) -> b x n", x=pieces)
    to = out[:, 0:(rows - DEC_T) * width].rearrange("b (x n) -> b x n", x=pieces)
    engine.dma_start(to[b], frm[b]).then_inc(done, 16)


def project(nc, d):
    with Phase(nc, "pj") as ph:
        gain = ph.sb("gain", [P, D])
        ident = ph.sb("ident", [P, P])
        scale = ph.sb("scale", [P, FBLK])
        x = ph.sb("x", [P, 2, D])
        square = ph.sb("square", [P, D])
        sumsq = ph.sb("sumsq", [P, 2])
        rms = ph.sb("rms", [P, 2])
        rstd = ph.sb("rstd", [P, 2])
        eps = ph.sb("eps", [P, 1])
        xn = ph.sb("xn", [P, 2, D])
        h_hi = ph.sb("h_hi", [P, DBLK, TOK], F32R)
        h_lo = ph.sb("h_lo", [P, DBLK, TOK], F32R)
        w = ph.sb("w", [P, 2, DBLK, P])
        w_hi = ph.sb("w_hi", [P, 2, DBLK, P], F32R)
        w_lo = ph.sb("w_lo", [P, 2, DBLK, P], F32R)
        proj = ph.sb("proj", [P, 2, TOK])
        turned = ph.banks("turned", 2)
        acc = ph.banks("acc", NGRP)

        const_in = ph.sem("const_in")
        x_in = ph.sems("x_in", 2)
        w_in = ph.sems("w_in", 2)
        squared = ph.sem("squared")
        eps_ready = ph.sem("eps_ready")
        rms_ready = ph.sem("rms_ready")
        rstd_ready = ph.sem("rstd_ready")
        xn_ready = ph.sem("xn_ready")
        turned_ready = ph.sem("turned_ready")
        hi_ready = ph.sem("hi_ready")
        lo_ready = ph.sem("lo_ready")
        w_hi_ready = ph.sem("w_hi_ready")
        w_lo_ready = ph.sem("w_lo_ready")
        acc_ready = ph.sem("acc_ready")
        even_out = ph.sem("even_out")
        odd_out = ph.sem("odd_out")
        stored = ph.sems("stored", 2)

        xp = d["x_prompt"].rearrange("b (n p) c -> (b n) p c", p=P)
        xs = d["x_sample"].rearrange("b t c -> (b t) c")
        wv = d["w_in"].rearrange("l (k p) (f m) -> (l f) p k m", p=P, m=P)
        pt = d["pt"]

        block = ph.block()

        @block.sync
        def _(sp):
            sp.dma_start(gain[:], d["g_mix_pre"].partition_broadcast(P)).then_inc(const_in, 16)
            sp.dma_start(ident[:], d["c_ident"]).then_inc(const_in, 16)
            sp.dma_start(scale[:], d["c_scale"]).then_inc(const_in, 16)
            with sp.Fori(0, TILES // 2) as it:
                for s in range(2):
                    sp.wait_ge(xn_ready, it * 2 + s + 1)
                    sp.dma_start(x[:, s, :], xp[it * 2 + s]).then_inc(x_in[s], 16)
            sp.wait_ge(xn_ready, TILES + 1)
            sp.dma_start(x[0:DEC, 0, :], xs).then_inc(x_in[0], 16)

            def load_w(f, s):
                sp.wait_ge(w_lo_ready, f + 1)
                sp.dma_start(w[:, s, :, :], wv[f]).then_inc(w_in[s], 16)

            def store_proj(f, s):
                sp.wait_ge(even_out, (f + 2) * (NGRP // 2))
                sp.wait_ge(odd_out, (f + 2) * (NGRP // 2))
                sp.dma_start(pt[f], proj[:, s, :]).then_inc(stored[s], 16)

            load_w(0, 0)
            load_w(1, 1)
            with sp.Fori(0, FBLK // 2 - 1) as it:
                for s in range(2):
                    store_proj(it * 2 + s, s)
                    load_w(it * 2 + (s + 2), s)
            for s in range(2):
                store_proj(FBLK - 2 + s, s)
            for s in range(2):
                sp.wait_ge(stored[s], 16 + 16 * FBLK // 2)

        @block.scalar
        def _(act):
            for s in range(2):
                act.sem_inc(stored[s], 16)
            act.sem_inc(even_out, NGRP // 2)

            def square_tile(t, s, k, n):
                act.wait_ge(x_in[s], k * 16 + 16)
                act.wait_ge(squared, t)
                nc.scalar.activation(square[0:n, :], x[0:n, s, :], ACT.Square, scale=D ** -0.5,
                                     accum_out=sumsq[0:n, s:s + 1]).then_inc(squared, 1)
                act.wait_ge(squared, t + 1)
                act.wait_ge(xn_ready, t + 1)
                nc.scalar.activation(rms[0:n, s:s + 1], sumsq[0:n, s:s + 1], ACT.Sqrt,
                                     bias=eps[0:n, :]).then_inc(rms_ready, 1)

            act.wait_ge(eps_ready, 1)

            def hi_tile(t, tok0, n):
                for half in range(2):
                    act.wait_ge(turned_ready, t * 2 + half + 1)
                    src = turned[half][:, :].rearrange("p (k m) -> p k m", m=P)
                    nc.scalar.copy(h_hi[:, 4 * half:4 * half + 4, bass.ds(tok0, n)],
                                   src[:, :, 0:n]).then_inc(hi_ready, 1)

            square_tile(0, 0, 0, P)
            with act.Fori(0, TILES // 2 - 1) as it:
                square_tile(it * 2 + 1, 1, it, P)
                hi_tile(it * 2, it * 2 * P, P)
                square_tile(it * 2 + 2, 0, it + 1, P)
                hi_tile(it * 2 + 1, (it * 2 + 1) * P, P)
            square_tile(TILES - 1, 1, TILES // 2 - 1, P)
            hi_tile(TILES - 2, (TILES - 2) * P, P)
            square_tile(TILES, 0, TILES // 2, DEC)
            hi_tile(TILES - 1, (TILES - 1) * P, P)
            hi_tile(TILES, SEQ, DEC)

            def split_hi(f, s, k):
                act.wait_ge(w_in[s], k * 16 + 16)
                act.wait_ge(acc_ready, (f + 1) * NGRP)
                nc.scalar.copy(w_hi[:, s, :, :], w[:, s, :, :]).then_inc(w_hi_ready, 1)

            def copy_even(f, s, k):
                act.wait_ge(stored[s], k * 16 + 16)
                for g in range(0, NGRP, 2):
                    act.wait_ge(acc_ready, (f + 2) * NGRP + g + 1)
                    apart(act)
                    nc.scalar.activation(proj[:, s, g * GRP:(g + 1) * GRP], acc[g][:, 0:GRP], ACT.Copy,
                                         scale=scale[:, bass.ds(f, 1)]).then_inc(even_out, 1)

            act.wait_ge(const_in, 48)
            split_hi(0, 0, 0)
            with act.Fori(0, FBLK // 2 - 1) as it:
                split_hi(it * 2 + 1, 1, it)
                copy_even(it * 2, 0, it)
                split_hi(it * 2 + 2, 0, it + 1)
                copy_even(it * 2 + 1, 1, it)
            split_hi(FBLK - 1, 1, FBLK // 2 - 1)
            copy_even(FBLK - 2, 0, FBLK // 2 - 1)
            copy_even(FBLK - 1, 1, FBLK // 2 - 1)

        @block.vector
        def _(dve):
            nc.vector.memset(eps[:], EPS).then_inc(eps_ready, 1)
            dve.sem_inc(xn_ready, 2)
            dve.sem_inc(lo_ready, 2)
            dve.sem_inc(w_lo_ready, 2)
            dve.sem_inc(odd_out, NGRP // 2)
            dve.wait_ge(const_in, 48)

            def normalise(t, s, n):
                dve.wait_ge(rms_ready, t + 1)
                nc.vector.reciprocal(rstd[0:n, s:s + 1], rms[0:n, s:s + 1]).then_inc(rstd_ready, 1)
                dve.wait_ge(rstd_ready, t + 1)
                dve.wait_ge(turned_ready, t * 2)
                nc.vector.scalar_tensor_tensor(xn[0:n, s, :], x[0:n, s, :], rstd[0:n, s:s + 1], gain[0:n, :],
                                               ALU.mult, ALU.mult).then_inc(xn_ready, 1)

            def lo_tile(t, tok0, n):
                for half in range(2):
                    dve.wait_ge(hi_ready, t * 2 + half + 1)
                    src = turned[half][:, :].rearrange("p (k m) -> p k m", m=P)
                    at = (slice(None), slice(4 * half, 4 * half + 4), bass.ds(tok0, n))
                    nc.vector.tensor_tensor(h_lo[at], src[:, :, 0:n], f32(h_hi[at]), ALU.subtract).then_inc(lo_ready, 1)

            normalise(0, 0, P)
            with dve.Fori(0, TILES // 2 - 1) as it:
                for s in range(2):
                    lo_tile(it * 2 + s, (it * 2 + s) * P, P)
                    normalise(it * 2 + s + 1, 1 - s, P)
            lo_tile(TILES - 2, (TILES - 2) * P, P)
            normalise(TILES - 1, 1, P)
            lo_tile(TILES - 1, (TILES - 1) * P, P)
            normalise(TILES, 0, DEC)
            lo_tile(TILES, SEQ, DEC)

            def split_lo(f, s):
                dve.wait_ge(w_hi_ready, f + 1)
                nc.vector.tensor_tensor(w_lo[:, s, :, :], w[:, s, :, :], f32(w_hi[:, s, :, :]),
                                        ALU.subtract).then_inc(w_lo_ready, 1)

            def copy_odd(f, s, k):
                dve.wait_ge(stored[s], k * 16 + 16)
                for g in range(1, NGRP, 2):
                    dve.wait_ge(acc_ready, (f + 2) * NGRP + g + 1)
                    nc.vector.tensor_scalar(proj[:, s, g * GRP:(g + 1) * GRP], acc[g][:, 0:GRP],
                                            scale[:, bass.ds(f, 1)], None, ALU.mult).then_inc(odd_out, 1)

            split_lo(0, 0)
            with dve.Fori(0, FBLK // 2 - 1) as it:
                split_lo(it * 2 + 1, 1)
                copy_odd(it * 2, 0, it)
                split_lo(it * 2 + 2, 0)
                copy_odd(it * 2 + 1, 1, it)
            split_lo(FBLK - 1, 1)
            copy_odd(FBLK - 2, 0, FBLK // 2 - 1)
            copy_odd(FBLK - 1, 1, FBLK // 2 - 1)

        @block.tensor
        def _(pe):
            pe.sem_inc(acc_ready, 2 * NGRP)
            pe.wait_ge(const_in, 48)

            def turn(t, s, n):
                pe.wait_ge(xn_ready, t + 3)
                for half in range(2):
                    pe.wait_ge(lo_ready, t * 2 + half + 1)
                    for j in range(4):
                        k = 4 * half + j
                        last = pe.transpose(turned[half][:, j * P:j * P + n], xn[0:n, s, k * P:(k + 1) * P],
                                            ident[0:n, 0:n])
                    last.then_inc(turned_ready, 1)

            with pe.Fori(0, TILES // 2) as it:
                for s in range(2):
                    turn(it * 2 + s, s, P)
            turn(TILES, 0, DEC)

            pe.wait_ge(lo_ready, 2 + 2 * (TILES + 1))
            with pe.Fori(0, FBLK // 2) as it:
                for s in range(2):
                    f = it * 2 + s
                    pe.wait_ge(w_lo_ready, f + 3)
                    for g in range(NGRP):
                        pe.wait_ge(odd_out if g % 2 else even_out, (f + 1 - 1) * (NGRP // 2) + g // 2 + 1)
                        cols = slice(g * GRP, (g + 1) * GRP)
                        for k in range(DBLK):
                            pe.matmul(acc[g][:, 0:GRP], w_hi[:, s, k, :], h_hi[:, k, cols], start=(k == 0), stop=False)
                            pe.matmul(acc[g][:, 0:GRP], w_hi[:, s, k, :], h_lo[:, k, cols], start=False, stop=False)
                            last = pe.matmul(acc[g][:, 0:GRP], w_lo[:, s, k, :], h_hi[:, k, cols], start=False,
                                             stop=(k == DBLK - 1))
                        last.then_inc(acc_ready, 1)


GR = PAST + DEC_T + 2 * P - 1
A_COLS = SEQ + P
A_FIRST = A_COLS - 2 * P
B_COLS = 4 * P
B_FIRST = B_COLS - 2 * P
A_AT = DEC_T
B_AT = DEC_T + A_COLS - B_COLS


def bucket_rows(window_counts):
    distance = PAST + DEC_T - 1 - np.arange(GR)
    exact = BUCKETS // 2
    scaled = np.log(np.maximum(distance, 1).astype(np.float32) / np.float32(exact)) / np.float32(math.log(2048 / exact))
    large = np.minimum(exact + (scaled * np.float32(BUCKETS - exact)).astype(np.int32), BUCKETS - 1)
    bucket = np.where(distance < exact, np.maximum(distance, 0), large)
    rows = np.zeros((BUCKETS + 1, GR), np.float32)
    count = window_counts(distance)
    seen = count > 0
    rows[bucket[seen], np.nonzero(seen)[0]] = 1.0
    rows[BUCKETS] = np.where(seen, np.log(np.maximum(count, 1).astype(np.float32)), np.float32(MASKED))
    return rows


def a_counts(distance):
    return sum(((distance >= 0) & (distance <= w) & (distance % s == 0)).astype(np.int32)
               for w, s in ((128, 1), (512, 4), (2048, 16)))


def b_counts(distance):
    return ((distance >= 0) & (distance <= BWIN)).astype(np.int32)


def rows_and_tables(nc, d):
    KV = 8
    with Phase(nc, "rt") as ph:
        ident = ph.sb("ident", [P, P])
        kv_t = ph.sb("kv_t", [P, 2, KV, P])
        kv = ph.sb("kv", [P, 2, KV * P])
        gates = ph.sb("gates", [P, 6, TOK])
        u = ph.sb("u", [P, 2, SEQ + 2])
        u_dec = ph.sb("u_dec", [P, 2, DEC_B, DEC_T + 2])
        conv = ph.sb("conv", [P, 2, TOK])
        taps = ph.sb("taps", [P, 2, 3])
        state = ph.sb("state", [2 * DEC_B + 3, CW])
        ends = ph.sb("ends", [P, 2, 2 + 2 * DEC_B])
        ends_rows = ph.sb("ends_rows", [2 + 2 * DEC_B, CW])
        table = ph.sb("table", [BUCKETS + 1, AH + BH])
        onehot = ph.sb("onehot", [BUCKETS + 1, 2, GR])
        source = ph.sb("source", [AH, 2, GR])
        turned = ph.banks("turned", 4)
        wide = ph.banks("wide", 3)
        small = ph.banks("small", 1)[0]

        const_in = ph.sem("const_in")
        kv_in = ph.sems("kv_in", 2)
        turned_ready = ph.sem("turned_ready")
        k_rows = ph.sem("k_rows")
        v_rows = ph.sem("v_rows")
        kv_out = ph.sems("kv_out", 2)
        gates_in = ph.sem("gates_in")
        state_turned = ph.sem("state_turned")
        conv_step = ph.sem("conv_step")
        ends_ready = ph.sem("ends_ready")
        ends_turned = ph.sem("ends_turned")
        ends_copied = ph.sem("ends_copied")
        conv_out = ph.sem("conv_out")
        table_ones = ph.sem("table_ones")
        table_in = ph.sem("table_in")
        source_mm = ph.sem("source_mm")
        source_sb = ph.sem("source_sb")
        source_out = ph.sem("source_out")
        spread_out = ph.sem("spread_out")

        GCH = [(c, min(512, GR - c)) for c in range(0, GR, 512)]
        block = ph.block()
        pt_k = d["pt"].rearrange("f p t -> p f t")

        @block.sync
        def _(sp):
            sp.dma_start(table[0:BUCKETS, :], d["rel_bias"]).then_inc(table_in, 16)
            sp.dma_start(onehot[:, 0, :], d["c_bucket_a"]).then_inc(table_in, 16)
            sp.dma_start(onehot[:, 1, :], d["c_bucket_b"]).then_inc(table_in, 16)
            sp.dma_start(ident[:], d["c_ident"]).then_inc(const_in, 16)

            def load_kv(t, tok0, s, n):
                sp.wait_ge(v_rows, t + 1)
                sp.wait_ge(k_rows, t + 1)
                sp.dma_start(kv_t[:, s, 0:6, 0:n], pt_k[:, AK0:AK0 + 6, bass.ds(tok0, n)]).then_inc(kv_in[s], 16)
                sp.dma_start(kv_t[:, s, 6:8, 0:n], pt_k[:, BK0:BK0 + 2, bass.ds(tok0, n)]).then_inc(kv_in[s], 16)

            with sp.Fori(0, TILES // 2) as it:
                for s in range(2):
                    load_kv(it * 2 + s, (it * 2 + s) * P, s, P)
            load_kv(TILES, SEQ, 0, DEC)

        @block.gpsimd
        def _(pool):
            pool.wait_ge(source_sb, 2 * len(GCH))
            pool.dma_start(d["source"].rearrange("b h x -> h b x"), source[:]).then_inc(source_out, 16)
            pool.wait_ge(source_out, 16)
            for b, first in ((0, A_AT), (1, B_AT)):
                for h in range(AH):
                    frm = bass.AP(d["source"].tensor, (b * AH + h) * GR + first, [[0, P], [1, GR - first]])
                    pool.dma_start(d["spread"][b, h, :, first:], frm).then_inc(spread_out, 16)
            pool.wait_ge(spread_out, 16 * 2 * AH)

        @block.scalar
        def _(act):
            act.sem_inc(k_rows, 2)
            act.dma_start(gates[:], pt_k[:, CB0:CB0 + 6, :]).then_inc(gates_in, 16)
            act.dma_start(state[0:2 * DEC_B, :], d["state_conv"].rearrange("l b j c -> (l b j) c")).then_inc(gates_in, 16)
            act.dma_start(state[2 * DEC_B:, :], d["conv_w"].rearrange("l j c -> (l j) c")).then_inc(gates_in, 16)

            N_STORES = 3
            for s in range(2):
                act.sem_inc(kv_out[s], 16 * N_STORES)

            def k_tile(t, k, s, n):
                act.wait_ge(turned_ready, t * 2 + 1)
                act.wait_ge(kv_out[s], (k + 1) * 16 * N_STORES)
                nc.scalar.copy(kv[0:n, s, 0:512], turned[2 * s][0:n, :]).then_inc(k_rows, 1)

            def store_tile(t, s):
                act.wait_ge(k_rows, t + 3)
                act.wait_ge(v_rows, t + 3)
                act.dma_start(d["kv"][bass.ds(t * P, P), 2 * AW + KVW:], kv[:, s, 2 * AW + KVW:]).then_inc(kv_out[s], 16)
                rows = lambda o: o.rearrange("l b (n p) h e -> (l b n) p (h e)", p=P)
                act.dma_start(rows(d["o_a_k_p"])[t], kv[:, s, 0:AW]).then_inc(kv_out[s], 16)
                act.dma_start(rows(d["o_a_v_p"])[t], kv[:, s, AW:2 * AW]).then_inc(kv_out[s], 16)

            with act.Fori(0, TILES // 2) as it:
                for s in range(2):
                    k_tile(it * 2 + s, it, s, P)
                    store_tile(it * 2 + s, s)
            last = kv[:, 1, :]
            act.dma_start(d["o_b_k_p"].rearrange("l b t h e -> (l b t) (h e)"), last[:, 6 * P:7 * P]).then_inc(kv_out[1], 16)
            act.dma_start(d["o_b_v_p"].rearrange("l b t h e -> (l b t) (h e)"), last[:, 7 * P:8 * P]).then_inc(kv_out[1], 16)
            k_tile(TILES, TILES // 2, 0, DEC)
            act.wait_ge(k_rows, TILES + 3)
            act.wait_ge(v_rows, TILES + 3)
            act.dma_start(d["kv"][SEQ:TOK, :], kv[0:DEC, 0, :]).then_inc(kv_out[0], 16)
            for b in range(DEC_B):
                new = kv[b * DEC_T:(b + 1) * DEC_T, 0, :]
                for out, c0, w, n in ((d["o_a_k_s"], 0, AW, PAST), (d["o_a_v_s"], AW, AW, PAST),
                                      (d["o_b_k_s"], 2 * AW, KVW, BWIN), (d["o_b_v_s"], 2 * AW + KVW, KVW, BWIN)):
                    dst = out[0, b].rearrange("t h e -> t (h e)")[n - DEC_T:n, :]
                    act.dma_start(dst, new[:, c0:c0 + w]).then_inc(kv_out[0], 16)
            act.wait_ge(conv_step, 14)
            act.dma_start(d["oct"].rearrange("c p t -> p c t"), conv[:]).then_inc(conv_out, 16)
            act.wait_ge(ends_turned, 1)
            nc.scalar.copy(ends_rows[:], small[0:2 + 2 * DEC_B, 64:64 + CW]).then_inc(ends_copied, 1)
            act.wait_ge(ends_copied, 1)
            act.dma_start(d["o_conv_p"].rearrange("l b j c -> (l b j) c"), ends_rows[0:2, :]).then_inc(conv_out, 16)
            act.dma_start(d["o_conv_s"].rearrange("l b j c -> (l b j) c"), ends_rows[2:, :]).then_inc(conv_out, 16)
            act.wait_ge(conv_out, 48)
            act.wait_ge(kv_out[0], 16 * (N_STORES * (TILES // 2 + 1) + 1 + 4 * DEC_B))
            act.wait_ge(kv_out[1], 16 * (N_STORES * (TILES // 2 + 1) + 2))

        @block.vector
        def _(dve):
            dve.sem_inc(v_rows, 2)
            nc.vector.memset(table[BUCKETS:BUCKETS + 1, :], 1.0).then_inc(table_ones, 1)

            for b in range(2):
                for i, (c, n) in enumerate(GCH):
                    dve.wait_ge(source_mm, b * len(GCH) + i + 1)
                    nc.vector.tensor_copy(source[:, b, c:c + n],
                                          wide[(b * len(GCH) + i) % 3][0:AH, 0:n]).then_inc(source_sb, 1)

            def v_tile(t, k, s, n):
                dve.wait_ge(turned_ready, t * 2 + 2)
                dve.wait_ge(kv_out[s], (k + 1) * 48)
                nc.vector.tensor_copy(kv[0:n, s, 512:1024], turned[2 * s + 1][0:n, :]).then_inc(v_rows, 1)

            with dve.Fori(0, TILES // 2) as it:
                for s in range(2):
                    v_tile(it * 2 + s, it, s, P)
            v_tile(TILES, TILES // 2, 0, DEC)

            dve.wait_ge(gates_in, 48)
            nc.vector.memset(u[:, :, 0:2], 0.0).then_inc(conv_step, 1)
            nc.vector.tensor_tensor(u[:, :, 2:], gates[:, 2:4, 0:SEQ], gates[:, 4:6, 0:SEQ],
                                    ALU.mult).then_inc(conv_step, 1)
            dve.wait_ge(state_turned, 1)
            turned_state = small[:, 0:64].rearrange("p (c x) -> p c x", c=2)
            for c in range(2):
                nc.vector.tensor_copy(u_dec[:, c, :, 0:2], turned_state[:, c, 0:2 * DEC_B].rearrange(
                    "p (b j) -> p b j", j=2)).then_inc(conv_step, 1)
            nc.vector.tensor_copy(taps[:], turned_state[:, :, 2 * DEC_B:2 * DEC_B + 3]).then_inc(conv_step, 1)
            for c in range(2):
                nc.vector.tensor_tensor(u_dec[:, c, :, 2:], gates[:, 2 + c, SEQ:].rearrange("p (b t) -> p b t", b=DEC_B),
                                        gates[:, 4 + c, SEQ:].rearrange("p (b t) -> p b t", b=DEC_B),
                                        ALU.mult).then_inc(conv_step, 1)
            dve.wait_ge(conv_step, 7)
            nc.vector.tensor_copy(ends[:, :, 0:2], u[:, :, SEQ:]).then_inc(ends_ready, 1)
            for c in range(2):
                nc.vector.tensor_copy(ends[:, c, 2:].rearrange("p (b j) -> p b j", j=2),
                                      u_dec[:, c, :, DEC_T:]).then_inc(ends_ready, 1)
            steps = 7
            for j in range(3):
                for c in range(2):
                    dst = [(conv[:, c, 0:SEQ], u[:, c, j:j + SEQ]),
                           (conv[:, c, SEQ:].rearrange("p (b t) -> p b t", b=DEC_B), u_dec[:, c, :, j:j + DEC_T])]
                    for to, frm in dst:
                        if j == 0:
                            last = nc.vector.tensor_scalar(to, frm, taps[:, c, j:j + 1], None, ALU.mult)
                        else:
                            last = nc.vector.scalar_tensor_tensor(to, frm, taps[:, c, j:j + 1], to, ALU.mult, ALU.add)
                    last.then_inc(conv_step, 1)
                steps += 2
                dve.wait_ge(conv_step, steps)
            nc.vector.tensor_tensor(conv[:], conv[:], gates[:, 0:2, :], ALU.mult).then_inc(conv_step, 1)

        @block.tensor
        def _(pe):
            pe.wait_ge(table_ones, 1)
            pe.wait_ge(table_in, 48)
            for b in range(2):
                for i, (c, n) in enumerate(GCH):
                    g = b * len(GCH) + i
                    if g >= 3:
                        pe.wait_ge(source_sb, g - 2)
                    pe.matmul(wide[g % 3][0:AH, 0:n], table[:, b * AH:(b + 1) * AH], onehot[:, b, c:c + n],
                              start=True, stop=True).then_inc(source_mm, 1)
            pe.wait_ge(const_in, 16)
            pe.wait_ge(gates_in, 48)
            for c in range(2):
                last = pe.transpose(small[:, c * 32:c * 32 + 2 * DEC_B + 3], state[:, c * P:(c + 1) * P],
                                    ident[0:2 * DEC_B + 3, 0:2 * DEC_B + 3])
            last.then_inc(state_turned, 1)

            def turn(t, k, s, n):
                pe.wait_ge(kv_in[s], 32 * k + 32)
                for half in range(2):
                    pe.wait_ge(v_rows if half else k_rows, t + 1)
                    for j in range(4):
                        last = pe.transpose(turned[2 * s + half][0:n, j * P:(j + 1) * P], kv_t[:, s, 4 * half + j, 0:n],
                                            ident[:, :])
                    last.then_inc(turned_ready, 1)

            with pe.Fori(0, TILES // 2) as it:
                for s in range(2):
                    turn(it * 2 + s, it, s, P)
            turn(TILES, TILES // 2, 0, DEC)
            pe.wait_ge(ends_ready, 3)
            for c in range(2):
                last = pe.transpose(small[0:2 + 2 * DEC_B, 64 + c * P:64 + (c + 1) * P], ends[:, c, :], ident[:, :])
            last.then_inc(ends_turned, 1)


def attend(nc, d, group):
    is_b = group == "b"
    ORDER = (0, 2, 4, 6, 7, 5, 3, 1)
    PAIRS = len(ORDER)
    UNITS = 2 * PAIRS
    COLS, FIRST = (B_COLS, B_FIRST) if is_b else (A_COLS, A_FIRST)
    KMAX = 3 * P if is_b else SEQ

    def key_blocks(u):
        p = ORDER[u % PAIRS]
        return range(max(2 * p - 1, 0) if is_b else 0, 2 * p + 2)

    def chunks(u):
        n = len(key_blocks(u)) * P
        return [(q, c, min(512, n - c), c // 512) for q in range(2) for c in range(0, n, 512)]

    def turns(u):
        n = len(key_blocks(u))
        return [range(j, min(j + 2, n)) for j in range(0, n, 2)]

    def chunks_before(u):
        return sum(len(chunks(x)) for x in range(u))

    def turns_before(u):
        return sum(len(turns(x)) for x in range(u))

    S_BANKS, T_BANKS = 2, 3
    P_SLOTS, LAG = 4, 2
    NCH, NTURN = chunks_before(UNITS), turns_before(UNITS)

    with Phase(nc, f"at{group}") as ph:
        ident = ph.sb("ident", [P, P])
        fold = ph.sb("fold", [P, P])
        q_raw = ph.sb("q_raw", [P, 2, SEQ])
        k_raw = ph.sb("k_raw", [P, 2, SEQ])
        v_raw = ph.sb("v_raw", [P, 2, TILES, HD])
        q2 = ph.sb("q2", [P, 2, SEQ], F32R)
        k_hi = ph.sb("k_hi", [P, 2, SEQ], F32R)
        k_lo = ph.sb("k_lo", [P, 2, SEQ], F32R)
        v2 = ph.sb("v2", [P, 2, TILES, 2, HD], F32R)
        bias = ph.sb("bias", [P, 2, COLS])
        prob = ph.sb("prob", [P, 3, 2, KMAX])
        top = ph.sb("top", [P, 3, 2, 4])
        minus_max = ph.sb("minus_max", [P, 3, 2])
        total = ph.sb("total", [P, 3, 2])
        sink = ph.sb("sink", [P, 2])
        sink_exp = ph.sb("sink_exp", [P, 3, 2])
        denominator = ph.sb("denominator", [P, 2, 2])
        inverse = ph.sb("inverse", [P, 2, 2])
        p_hi = ph.sb("p_hi", [P, P_SLOTS, 512], F32R)
        p_lo = ph.sb("p_lo", [P, P_SLOTS, 512], F32R)
        o_t = ph.sb("o_t", [P, 2, 2 * P])
        o_rows = ph.sb("o_rows", [P, 2, TILES, HD])
        score_ps = ph.banks("score", S_BANKS)
        turn_ps = ph.banks("turn", T_BANKS)
        ot_ps = ph.banks("ot", 2)
        o_ps = ph.banks("o", 1)[0]

        const_in = ph.sem("const_in")
        q_in = ph.sems("q_in", 2)
        k_in = ph.sems("k_in", 2)
        v_in = ph.sems("v_in", 2)
        bias_in = ph.sems("bias_in", 2)
        q_split = ph.sem("q_split")
        k_split = ph.sem("k_split")
        v_split = ph.sem("v_split")
        scored = ph.sem("scored")
        biased = ph.sem("biased")
        max_ready = ph.sem("max_ready")
        exped = ph.sem("exped")
        turned = ph.sem("turned")
        hi_ready = ph.sem("hi_ready")
        lo_ready = ph.sem("lo_ready")
        weighed = ph.sem("weighed")
        ot_copied = ph.sem("ot_copied")
        folded = ph.sem("folded")
        sink_ready = ph.sem("sink_ready")
        summed = ph.sem("summed")
        inverted = ph.sem("inverted")
        out_ready = ph.sem("out_ready")
        stored = ph.sems("stored", 2)
        cache_out = ph.sem("cache_out")

        pt_rows = d["pt"].rearrange("f p t -> (f p) t")
        q_rows = pt_rows[(BQ0 if is_b else AQ0) * P:, :]
        k_rows = pt_rows[(BK0 if is_b else AK0) * P:, :]

        def q_head(it, s):
            return it + s * (BH // KVH) if is_b else it * 2 + s

        def k_head(it, s):
            return s if is_b else it * 2 + s

        v_rows = (bass.AP(d["kv"].tensor, 2 * AW + KVW, [[D, P], [P * D, TILES], [1, KVW]]) if is_b else
                  bass.AP(d["o_a_v_p"].tensor, 0, [[AW, P], [P * AW, TILES], [1, AW]]))
        mix_rows = bass.AP(d["mix"].tensor, 0, [[AW + BW, P], [P * (AW + BW), TILES], [1, AW + BW]])
        head0 = (AH if is_b else 0) * P * GR
        bias_rows = bass.AP(d["spread"].tensor, head0 + (B_AT if is_b else A_AT) + P - 1,
                            [[P * GR, AH], [GR - 1, P], [1, COLS]])

        block = ph.block()

        @block.sync
        def _(sp):
            sp.dma_start(ident[:], d["c_ident"]).then_inc(const_in, 16)
            sp.dma_start(fold[:], d["c_fold"]).then_inc(const_in, 16)

            def load(it, s, first):
                q_row, k_row, v_col = q_head(it, s) * HD, k_head(it, s) * HD, k_head(it, s) * HD
                kv_heads = not is_b or first
                for half in range(2):
                    to = slice(half * HD, (half + 1) * HD)
                    if not first and not half:
                        sp.wait_ge(q_split, it * 4 + 2 * s - 2)
                        apart(sp)
                    sp.dma_start(q_raw[to, s, :], q_rows[bass.ds(q_row, HD), 0:SEQ]).then_inc(q_in[s], 16)
                if kv_heads:
                    for half in range(2):
                        to = slice(half * HD, (half + 1) * HD)
                        if not first and not half:
                            sp.wait_ge(k_split, it * 4 + 2 * s - 2)
                            apart(sp)
                        sp.dma_start(k_raw[to, s, :], k_rows[bass.ds(k_row, HD), 0:SEQ]).then_inc(k_in[s], 16)
                    if not first:
                        sp.wait_ge(v_split, it * 4 + 2 * s - 2)
                        apart(sp)
                    sp.dma_start(v_raw[:, s, :, :], v_rows[:, :, bass.ds(v_col, HD)]).then_inc(v_in[s], 16)
                if not first:
                    sp.wait_ge(biased, S_BANKS + (it - 1) * NCH + chunks_before(PAIRS * (s + 1)))
                    apart(sp)
                if is_b:
                    if not first:
                        sp.wait_ge(out_ready, (it - 1) * UNITS + PAIRS * (s + 1))
                        apart(sp)
                    sp.dma_start(sink[:, s:s + 1],
                                 d["b_sinks"][:, bass.ds(q_head(it, s), 1)].partition_broadcast(P)).then_inc(bias_in[s], 16)
                sp.dma_start(bias[:, s, :], bias_rows[q_head(it, s)]).then_inc(bias_in[s], 16)

            def store(it, s):
                sp.wait_ge(out_ready, it * UNITS + PAIRS * (s + 1))
                apart(sp)
                col = (AW if is_b else 0) + q_head(it, s) * HD
                sp.dma_start(mix_rows[:, :, bass.ds(col, HD)], o_rows[:, s, :, :]).then_inc(stored[s], 16)

            load(0, 0, True)
            load(0, 1, True)
            with sp.Fori(1, AH // 2) as it:
                for s in range(2):
                    load(it, s, False)
                    store(it - 1, s)
            for s in range(2):
                store(AH // 2 - 1, s)
            for s in range(2):
                sp.wait_ge(stored[s], 16 + 16 * (AH // 2))

        @block.gpsimd
        def _(pool):
            pool.sem_inc(weighed, NTURN)

            def split_k(it, s):
                pool.wait_ge(k_in[s], it * 32 + 32)
                pool.wait_ge(scored, (it - 1) * NCH + chunks_before(PAIRS * (s + 1)))
                apart(pool)
                nc.gpsimd.tensor_copy(k_hi[:, s, :], k_raw[:, s, :]).then_inc(k_split, 1)
                pool.wait_ge(k_split, it * 4 + 2 * s + 1)
                apart(pool)
                nc.gpsimd.tensor_tensor(k_lo[:, s, :], k_raw[:, s, :], f32(k_hi[:, s, :]), ALU.subtract).then_inc(k_split, 1)

            def split_q(it, s):
                pool.wait_ge(q_in[s], it * 32 + 32)
                pool.wait_ge(scored, (it - 1) * NCH + chunks_before(PAIRS * (s + 1)))
                apart(pool)
                nc.gpsimd.tensor_copy(q2[:, s, :], q_raw[:, s, :]).then_inc(q_split, 1)
                pool.wait_ge(q_split, it * 4 + 2 * s + 1)
                if not is_b:
                    pool.wait_ge(k_split, it * 4 + 2 * s + 2)
                apart(pool)
                nc.gpsimd.tensor_tensor(q2[HD:P, s, :], q_raw[HD:P, s, :], f32(q2[HD:P, s, :]),
                                        ALU.subtract).then_inc(q_split, 1)
                pool.wait_ge(q_split, it * 4 + 2 * s + 2)
                apart(pool)

            def split_v(it, s, first):
                pool.wait_ge(v_in[s], it * 16 + 16)
                if not first:
                    pool.wait_ge(weighed, it * NTURN + turns_before(PAIRS * (s + 1)))
                    apart(pool)
                nc.gpsimd.tensor_copy(v2[:, s, :, 0, :], v_raw[:, s, :, :]).then_inc(v_split, 1)
                pool.wait_ge(v_split, it * 4 + 2 * s + 1)
                if not first:
                    apart(pool)
                nc.gpsimd.tensor_tensor(v2[:, s, :, 1, :], v_raw[:, s, :, :], f32(v2[:, s, :, 0, :]),
                                        ALU.subtract).then_inc(v_split, 1)

            for s in range(2):
                split_v(0, s, True)
            with pool.Fori(1, AH // 2) as it:
                for s in range(2):
                    if not is_b:
                        split_k(it, s)
                    split_q(it, s)
                    if not is_b:
                        split_v(it, s, False)

        @block.tensor
        def _(pe):
            pe.wait_ge(const_in, 32)

            def score(it, u, i):
                s, p = u // PAIRS, ORDER[u % PAIRS]
                q, c, n, _ = chunks(u)[i]
                if i == 0 and u % PAIRS == 0:
                    pe.wait_ge(q_split, it * 4 + 2 * s + 2)
                    if is_b:
                        pe.wait_ge(k_split, 2 * s + 2)
                    else:
                        pe.wait_ge(k_split, it * 4 + 2 * s + 2)
                x = chunks_before(u) + i
                pe.wait_ge(biased, it * NCH + (x + 1 if x >= S_BANKS else S_BANKS))
                q0 = (2 * p + q) * P
                k0 = key_blocks(u)[0] * P + c
                out = score_ps[x % S_BANKS][:, 0:n]
                pe.matmul(out, q2[:, s, q0:q0 + P], k_hi[:, s, k0:k0 + n], start=True, stop=False)
                pe.matmul(out, q2[:, s, q0:q0 + P], k_lo[:, s, k0:k0 + n], start=False, stop=True).then_inc(scored, 1)

            def turn(it, u, g):
                if g == 0:
                    pe.wait_ge(exped, (it * UNITS + u + 1) * 2)
                x = turns_before(u) + g
                pe.wait_ge(lo_ready, it * NTURN + (x + 1 if x >= T_BANKS else T_BANKS))
                for slot, kb in enumerate(turns(u)[g]):
                    for q in range(2):
                        at = (slot * 2 + q) * P
                        last = pe.transpose(turn_ps[x % T_BANKS][:, at:at + P], prob[:, u % 3, q, kb * P:(kb + 1) * P], ident[:])
                last.then_inc(turned, 1)

            def weigh(it, u, g):
                s = u // PAIRS
                x = turns_before(u) + g
                if g == 0:
                    if u % PAIRS == 0:
                        if is_b:
                            pe.wait_ge(v_split, 2 * s + 2)
                        else:
                            pe.wait_ge(v_split, it * 4 + 2 * s + 2)
                    pe.wait_ge(ot_copied, it * UNITS + u + 1)
                pe.wait_ge(lo_ready, T_BANKS + it * NTURN + x + 1)
                n = len(key_blocks(u))
                for slot, kb in enumerate(turns(u)[g]):
                    vt = v2[:, s, key_blocks(u)[kb], :, :].rearrange("p a e -> p (a e)")
                    cols = slice(slot * 2 * P, (slot + 1) * 2 * P)
                    pe.matmul(ot_ps[u % 2][:, 0:2 * P], vt, p_hi[:, x % P_SLOTS, cols], start=(kb == 0), stop=False)
                    last = pe.matmul(ot_ps[u % 2][:, 0:2 * P], vt, p_lo[:, x % P_SLOTS, cols], start=False, stop=(kb == n - 1))
                last.then_inc(weighed, 1)

            def fold_rows(it, u):
                pe.wait_ge(ot_copied, 2 + it * UNITS + u + 1)
                pe.wait_ge(out_ready, it * UNITS + u)
                for q in range(2):
                    last = pe.matmul(o_ps[:, q * P:(q + 1) * P], o_t[:, u % 2, q * P:(q + 1) * P], fold[:], start=True,
                                     stop=True)
                last.then_inc(folded, 1)

            with pe.Fori(0, AH // 2) as it:
                for u in range(-2, UNITS + 1):
                    n_s = len(chunks(u + 2)) if u + 2 < UNITS else 0
                    n_t = len(turns(u)) if 0 <= u < UNITS else 0
                    lag = max(min(LAG, n_t), 1)
                    for i in range(max(n_s, n_t + lag)):
                        if i < n_t:
                            turn(it, u, i)
                        if i < n_s:
                            score(it, u + 2, i)
                        if i == 0 and u >= 1:
                            fold_rows(it, u - 1)
                        if lag <= i < n_t + lag and n_t:
                            weigh(it, u, i - lag)

        @block.scalar
        def _(act):
            act.sem_inc(ot_copied, 2)
            def split_hi(it, u, g):
                x = turns_before(u) + g
                act.wait_ge(turned, it * NTURN + x + 1)
                act.wait_ge(weighed, NTURN + it * NTURN + (x + 1 - P_SLOTS if x >= P_SLOTS else 0))
                n = len(turns(u)[g]) * 2 * P
                nc.scalar.copy(p_hi[:, x % P_SLOTS, 0:n], turn_ps[x % T_BANKS][:, 0:n]).then_inc(hi_ready, 1)

            def exp(it, u, q):
                n = len(key_blocks(u)) * P
                act.wait_ge(max_ready, it * UNITS + u + 1)
                if is_b and q == 0:
                    s = u // PAIRS
                    for i in range(2):
                        last = nc.scalar.activation(sink_exp[:, u % 3, i:i + 1], sink[:, s:s + 1], ACT.Exp,
                                                    bias=minus_max[:, u % 3, i:i + 1])
                    last.then_inc(sink_ready, 1)
                row = prob[:, u % 3, q, 0:n]
                nc.scalar.activation(row, row, ACT.Exp, bias=minus_max[:, u % 3, q:q + 1],
                                     accum_out=total[:, u % 3, q:q + 1]).then_inc(exped, 1)

            def copy_ot(it, u):
                act.wait_ge(weighed, NTURN + it * NTURN + turns_before(u + 1))
                if u >= 2:
                    act.wait_ge(folded, it * UNITS + u - 1)
                else:
                    act.wait_ge(folded, it * UNITS)
                nc.scalar.copy(o_t[:, u % 2, :], ot_ps[u % 2][:, 0:2 * P]).then_inc(ot_copied, 1)

            for s in range(2):
                for raw, hi, raw_in, split in ((q_raw, q2, q_in, q_split), (k_raw, k_hi, k_in, k_split)):
                    act.wait_ge(raw_in[s], 32)
                    act.wait_ge(split, 2 * s)
                    nc.scalar.copy(hi[:, s, :], raw[:, s, :]).then_inc(split, 1)
            if is_b:
                for b in range(DEC_B):
                    copy_cache(act, d["cache_b_k"], d["o_b_k_s"], b, 16, cache_out)
                    copy_cache(act, d["cache_b_v"], d["o_b_v_s"], b, 16, cache_out)

            with act.Fori(0, AH // 2) as it:
                for u in range(-1, UNITS):
                    n_t = len(turns(u)) if u >= 0 else 0
                    for i in range(max(n_t, 2)):
                        if i < n_t:
                            split_hi(it, u, i)
                        if i < 2 and u + 1 < UNITS:
                            exp(it, u + 1, i)
                    if u >= 0:
                        copy_ot(it, u)
            if is_b:
                act.wait_ge(cache_out, 16 * DEC_B * 2)

        @block.vector
        def _(dve):
            dve.sem_inc(biased, S_BANKS)
            dve.sem_inc(lo_ready, T_BANKS)
            for s in range(2):
                dve.sem_inc(stored[s], 16)

            def add_bias(it, u, i):
                s, p = u // PAIRS, ORDER[u % PAIRS]
                q, c, n, j = chunks(u)[i]
                x = chunks_before(u) + i
                if i == 0:
                    if u % PAIRS == 0:
                        dve.wait_ge(bias_in[s], (it + 1) * (32 if is_b else 16))
                    dve.wait_ge(turned, it * NTURN + (turns_before(u - 2) if u >= 3 else 0))
                dve.wait_ge(scored, it * NCH + x + 1)
                apart(dve)
                key = key_blocks(u)[0] * P + c
                at = key - (2 * p + q) * P + FIRST
                nc.vector.tensor_tensor_reduce(prob[:, u % 3, q, c:c + n], score_ps[x % S_BANKS][:, 0:n], bias[:, s, at:at + n],
                                               1.0, sink[:, s:s + 1] if is_b else MASKED, ALU.add, ALU.max,
                                               top[:, u % 3, q, j:j + 1]).then_inc(biased, 1)

            def maxima(it, u):
                dve.wait_ge(biased, S_BANKS + it * NCH + chunks_before(u + 1))
                dve.wait_ge(out_ready, it * UNITS + max(u - 3, 0))
                n = len(chunks(u)) // 2
                nc.vector.tensor_reduce(minus_max[:, u % 3, :], top[:, u % 3, :, 0:n], AX, ALU.max,
                                        negate=True).then_inc(max_ready, 1)

            def split_lo(it, u, g):
                x = turns_before(u) + g
                dve.wait_ge(hi_ready, it * NTURN + x + 1)
                n = len(turns(u)[g]) * 2 * P
                nc.vector.tensor_tensor(p_lo[:, x % P_SLOTS, 0:n], turn_ps[x % T_BANKS][:, 0:n], f32(p_hi[:, x % P_SLOTS, 0:n]),
                                        ALU.subtract).then_inc(lo_ready, 1)

            def finish(it, u):
                s, p = u // PAIRS, ORDER[u % PAIRS]
                denominators = total[:, u % 3, :]
                if is_b:
                    dve.wait_ge(sink_ready, it * UNITS + u + 1)
                    nc.vector.tensor_tensor(denominator[:, u % 2, :], total[:, u % 3, :], sink_exp[:, u % 3, :],
                                            ALU.add).then_inc(summed, 1)
                    dve.wait_ge(summed, it * UNITS + u + 1)
                    denominators = denominator[:, u % 2, :]
                nc.vector.reciprocal(inverse[:, u % 2, :], denominators).then_inc(inverted, 1)
                dve.wait_ge(inverted, it * UNITS + u + 1)
                if u % PAIRS == 0:
                    dve.wait_ge(stored[s], it * 16 + 16)
                dve.wait_ge(folded, it * UNITS + u + 1)
                for q in range(2):
                    last = nc.vector.tensor_scalar(o_rows[:, s, 2 * p + q, :], o_ps[:, q * P:q * P + HD],
                                                   inverse[:, u % 2, q:q + 1], None, ALU.mult)
                last.then_inc(out_ready, 1)

            for s in range(2):
                dve.wait_ge(q_split, 2 * s + 1)
                nc.vector.tensor_tensor(q2[HD:P, s, :], q_raw[HD:P, s, :], f32(q2[HD:P, s, :]),
                                        ALU.subtract).then_inc(q_split, 1)
                dve.wait_ge(k_split, 2 * s + 1)
                nc.vector.tensor_tensor(k_lo[:, s, :], k_raw[:, s, :], f32(k_hi[:, s, :]), ALU.subtract).then_inc(k_split, 1)

            with dve.Fori(0, AH // 2) as it:
                for u in range(-2, UNITS + 1):
                    n_s = len(chunks(u + 2)) if u + 2 < UNITS else 0
                    n_t = len(turns(u)) if 0 <= u < UNITS else 0
                    for i in range(max(n_s, n_t)):
                        if i < n_s:
                            add_bias(it, u + 2, i)
                        if i < n_t:
                            split_lo(it, u, i)
                    if u >= 1:
                        finish(it, u - 1)
                    if n_s:
                        maxima(it, u + 2)


def steps_of_tiles(engine, step):
    assert TILES == 16
    step(0, 0, 0)
    step(1, 1, 0)
    with engine.Fori(1, TILES // 2 - 1) as it:
        for s in range(2):
            step(it * 2 + s, s, it)
    for t in range(TILES - 2, TILES + 2):
        step(t, t % 2, t // 2)


def tile_rows(t):
    return DEC if isinstance(t, int) and t == TILES else P


def exists(t):
    return not isinstance(t, int) or 0 <= t <= TILES


def out_project(nc, d):
    with Phase(nc, "op") as ph:
        ident = ph.sb("ident", [P, P])
        eps = ph.sb("eps", [P, 1])
        gain_post = ph.sb("gain_post", [P, D])
        gain_pre = ph.sb("gain_pre", [P, D])
        w = ph.sb("w", [P, 2, D])
        w_hi = ph.sb("w_hi", [P, DBLK, D], F32R)
        w_lo = ph.sb("w_lo", [P, DBLK, D], F32R)
        mix = ph.sb("mix", [P, 2, AW + BW])
        conv = ph.sb("conv", [P, 2, 2, P])
        x = ph.sb("x", [P, 2, D])
        m_hi = ph.sb("m_hi", [P, 2, DBLK, P], F32R)
        m_lo = ph.sb("m_lo", [P, 2, DBLK, P], F32R)
        square = ph.sb("square", [P, D])
        sumsq = ph.sb("sumsq", [P, 2, 2])
        rms = ph.sb("rms", [P, 2, 2])
        rstd = ph.sb("rstd", [P, 2, 2])
        y = ph.sb("y", [P, D])
        x1 = ph.sb("x1", [P, 2, D])
        h = ph.sb("h", [P, 2, D])
        h_hi = ph.sb("h_hi", [P, 2, DBLK, P], F32R)
        h_lo = ph.sb("h_lo", [P, 2, DBLK, P], F32R)
        m_ps = ph.banks("m", 2)
        y_ps = [ph.ctx.enter_context(nc.psum_tensor(f"op_y{s}", [P, D], F32)) for s in range(2)]
        h_ps = ph.banks("h", 2)

        const_in = ph.sem("const_in")
        eps_ready = ph.sem("eps_ready")
        w_in = ph.sems("w_in", 2)
        w_hi_ready = ph.sem("w_hi_ready")
        w_lo_ready = ph.sem("w_lo_ready")
        mix_in = ph.sems("mix_in", 2)
        x_in = ph.sems("x_in", 2)
        m_turned = ph.sem("m_turned")
        m_hi_ready = ph.sem("m_hi_ready")
        m_lo_ready = ph.sem("m_lo_ready")
        y_ready = ph.sem("y_ready")
        squared = ph.sem("squared")
        rms_ready = ph.sem("rms_ready")
        dve_step = ph.sem("dve_step")
        h_turned = ph.sem("h_turned")
        h_hi_ready = ph.sem("h_hi_ready")
        h_lo_ready = ph.sem("h_lo_ready")
        x1_out = ph.sems("x1_out", 2)
        h_out = ph.sems("h_out", 2)

        xp = d["x_prompt"].rearrange("b (n p) c -> (b n) p c", p=P)
        xs = d["x_sample"].rearrange("b t c -> (b t) c")
        wv = d["w_out"].rearrange("l (k p) c -> (l k) p c", p=P)
        Y, X1, H = 2, 3, 5

        block = ph.block()

        @block.sync
        def _(sp):
            sp.dma_start(ident[:], d["c_ident"]).then_inc(const_in, 16)
            sp.dma_start(gain_post[:], d["g_mix_post"].partition_broadcast(P)).then_inc(const_in, 16)
            sp.dma_start(gain_pre[:], d["g_mlp_pre"].partition_broadcast(P)).then_inc(const_in, 16)

            def load_mix(t, s):
                sp.wait_ge(m_lo_ready, t * 3 + 3)
                n = tile_rows(t)
                sp.dma_start(mix[0:n, s, :], d["mix"][bass.ds(t * P, n), :]).then_inc(mix_in[s], 16)
                sp.dma_start(conv[:, s, :, 0:n],
                             d["oct"].rearrange("c p t -> p c t")[:, :, bass.ds(t * P, n)]).then_inc(mix_in[s], 16)

            def load_x(t, s):
                sp.wait_ge(dve_step, t * 5 + X1)
                n = tile_rows(t)
                sp.dma_start(x[0:n, s, :], xs if n == DEC else xp[t]).then_inc(x_in[s], 16)

            def store(t, s):
                n = tile_rows(t)
                sp.wait_ge(dve_step, 10 + t * 5 + X1)
                sp.dma_start(d["x1"][bass.ds(t * P, n), :], x1[0:n, s, :]).then_inc(x1_out[s], 16)
                sp.wait_ge(h_lo_ready, 4 + t * 2 + 2)
                apart(sp)
                for part, to in ((h_hi, d["h_hi"]), (h_lo, d["h_lo"])):
                    sp.dma_start(to.rearrange("k p t -> p k t")[:, :, bass.ds(t * P, n)],
                                 f32(part[:, s, :, 0:n])).then_inc(h_out[s], 16)

            load_mix(0, 0)
            load_x(0, 0)
            load_mix(1, 1)
            for k in range(DBLK):
                if k >= 2:
                    sp.wait_ge(w_lo_ready, k - 1)
                sp.dma_start(w[:, k % 2, :], wv[k]).then_inc(w_in[k % 2], 16)

            def step(t, s, k):
                if isinstance(t, int):
                    if t + 2 <= TILES:
                        load_mix(t + 2, s)
                    if t + 1 <= TILES:
                        load_x(t + 1, 1 - s)
                    if 1 <= t:
                        store(t - 1, 1 - s)
                else:
                    load_mix(t + 2, s)
                    load_x(t + 1, 1 - s)
                    store(t - 1, 1 - s)

            steps_of_tiles(sp, step)
            for s in range(2):
                sp.wait_ge(x1_out[s], 16 + 16 * (TILES // 2 + 1 - s))
                sp.wait_ge(h_out[s], 32 + 32 * (TILES // 2 + 1 - s))

        @block.tensor
        def _(pe):
            pe.sem_inc(y_ready, 2)
            pe.wait_ge(const_in, 48)

            def turn_mix(t, s, k):
                n = tile_rows(t)
                pe.wait_ge(mix_in[s], k * 32 + 32)
                for half, blocks in ((0, 4), (1, 2)):
                    pe.wait_ge(m_lo_ready, 3 + t * 3 + half + 1)
                    for j in range(blocks):
                        c = (4 * half + j) * P
                        last = pe.transpose(m_ps[half][:, j * P:j * P + n], mix[0:n, s, c:c + P], ident[0:n, 0:n])
                    last.then_inc(m_turned, 1)

            def product(t, s):
                n = tile_rows(t)
                pe.wait_ge(m_lo_ready, 6 + t * 3 + 3)
                pe.wait_ge(dve_step, t * 5 + Y)
                for k in range(DBLK):
                    if isinstance(t, int) and t == 0:
                        pe.wait_ge(w_lo_ready, k + 1)
                    for a, b in ((m_hi, w_hi), (m_hi, w_lo), (m_lo, w_hi)):
                        for half in range(2):
                            cols = slice(half * 512, half * 512 + 512)
                            last = pe.matmul(y_ps[s][0:n, cols], a[:, s, k, 0:n], b[:, k, cols],
                                             start=(k == 0 and a is m_hi and b is w_hi),
                                             stop=(k == DBLK - 1 and a is m_lo))
                last.then_inc(y_ready, 1)

            def turn_h(t, s):
                n = tile_rows(t)
                pe.wait_ge(dve_step, 10 + t * 5 + H)
                for half in range(2):
                    pe.wait_ge(h_lo_ready, 2 + t * 2 + half + 1)
                    for j in range(4):
                        c = (4 * half + j) * P
                        last = pe.transpose(h_ps[half][:, j * P:j * P + n], h[0:n, s, c:c + P], ident[0:n, 0:n])
                    last.then_inc(h_turned, 1)

            turn_mix(0, 0, 0)

            def step(t, s, k):
                if exists(t + 1):
                    turn_mix(t + 1, 1 - s, k + s)
                if exists(t):
                    product(t, s)
                if exists(t - 1):
                    turn_h(t - 1, 1 - s)

            steps_of_tiles(pe, step)

        @block.scalar
        def _(act):
            for s in range(2):
                act.sem_inc(x1_out[s], 16)
                act.sem_inc(h_out[s], 32)

            def hi_mix(t, s, k):
                n = tile_rows(t)
                act.wait_ge(y_ready, t + 1)
                for half, blocks in ((0, 4), (1, 2)):
                    act.wait_ge(m_turned, t * 2 + half + 1)
                    src = m_ps[half][:, 0:blocks * P].rearrange("p (k m) -> p k m", m=P)[:, :, 0:n]
                    nc.scalar.copy(m_hi[:, s, 4 * half:4 * half + blocks, 0:n], src).then_inc(m_hi_ready, 1)
                act.wait_ge(mix_in[s], k * 32 + 32)
                nc.scalar.copy(m_hi[:, s, 6:8, 0:n], conv[:, s, :, 0:n]).then_inc(m_hi_ready, 1)

            def rms_of(t, s, which, src):
                n = tile_rows(t)
                nc.scalar.activation(square[0:n, :], src, ACT.Square, scale=D ** -0.5,
                                     accum_out=sumsq[0:n, s, which:which + 1]).then_inc(squared, 1)
                act.wait_ge(squared, t * 2 + which + 1)
                nc.scalar.activation(rms[0:n, s, which:which + 1], sumsq[0:n, s, which:which + 1], ACT.Sqrt,
                                     bias=eps[0:n, :]).then_inc(rms_ready, 1)

            def hi_h(t, s, k):
                n = tile_rows(t)
                act.wait_ge(h_out[s], k * 32 + 32)
                for half in range(2):
                    act.wait_ge(h_turned, t * 2 + half + 1)
                    src = h_ps[half][:, :].rearrange("p (k m) -> p k m", m=P)[:, :, 0:n]
                    nc.scalar.copy(h_hi[:, s, 4 * half:4 * half + 4, 0:n], src).then_inc(h_hi_ready, 1)

            hi_mix(0, 0, 0)
            for k in range(DBLK):
                act.wait_ge(w_in[k % 2], 16 * (k // 2 + 1))
                nc.scalar.copy(w_hi[:, k, :], w[:, k % 2, :]).then_inc(w_hi_ready, 1)
            act.wait_ge(eps_ready, 1)

            def step(t, s, k):
                if exists(t + 1):
                    hi_mix(t + 1, 1 - s, k + s)
                if exists(t - 1):
                    hi_h(t - 1, 1 - s, k - 1 + s)
                if exists(t):
                    n = tile_rows(t)
                    act.wait_ge(y_ready, 2 + t + 1)
                    act.wait_ge(dve_step, t * 5 + H)
                    rms_of(t, s, 0, y_ps[s][0:n, :])
                    act.wait_ge(dve_step, 10 + t * 5 + X1)
                    rms_of(t, s, 1, x1[0:n, s, :])

            steps_of_tiles(act, step)

        @block.vector
        def _(dve):
            nc.vector.memset(eps[:], EPS).then_inc(eps_ready, 1)
            dve.sem_inc(m_lo_ready, 6)
            dve.sem_inc(dve_step, 10)
            dve.sem_inc(h_lo_ready, 4)
            dve.wait_ge(const_in, 48)

            def lo_mix(t, s):
                n = tile_rows(t)
                for half, blocks in ((0, 4), (1, 2)):
                    dve.wait_ge(m_hi_ready, t * 3 + half + 1)
                    src = m_ps[half][:, 0:blocks * P].rearrange("p (k m) -> p k m", m=P)[:, :, 0:n]
                    at = (slice(None), s, slice(4 * half, 4 * half + blocks), slice(0, n))
                    nc.vector.tensor_tensor(m_lo[at], src, f32(m_hi[at]), ALU.subtract).then_inc(m_lo_ready, 1)
                dve.wait_ge(m_hi_ready, t * 3 + 3)
                nc.vector.tensor_tensor(m_lo[:, s, 6:8, 0:n], conv[:, s, :, 0:n], f32(m_hi[:, s, 6:8, 0:n]),
                                        ALU.subtract).then_inc(m_lo_ready, 1)

            def lo_h(t, s):
                n = tile_rows(t)
                for half in range(2):
                    dve.wait_ge(h_hi_ready, t * 2 + half + 1)
                    src = h_ps[half][:, :].rearrange("p (k m) -> p k m", m=P)[:, :, 0:n]
                    at = (slice(None), s, slice(4 * half, 4 * half + 4), slice(0, n))
                    nc.vector.tensor_tensor(h_lo[at], src, f32(h_hi[at]), ALU.subtract).then_inc(h_lo_ready, 1)

            def rows(t, s, k):
                n = tile_rows(t)
                at = 10 + t * 5
                dve.wait_ge(rms_ready, t * 2 + 1)
                nc.vector.reciprocal(rstd[0:n, s, 0:1], rms[0:n, s, 0:1]).then_inc(dve_step, 1)
                dve.wait_ge(dve_step, at + 1)
                nc.vector.scalar_tensor_tensor(y[0:n, :], y_ps[s][0:n, :], rstd[0:n, s, 0:1], gain_post[0:n, :],
                                               ALU.mult, ALU.mult).then_inc(dve_step, 1)
                dve.wait_ge(dve_step, at + Y)
                dve.wait_ge(x_in[s], k * 16 + 16)
                dve.wait_ge(x1_out[s], k * 16 + 16)
                nc.vector.tensor_tensor(x1[0:n, s, :], y[0:n, :], x[0:n, s, :], ALU.add).then_inc(dve_step, 1)
                dve.wait_ge(rms_ready, t * 2 + 2)
                nc.vector.reciprocal(rstd[0:n, s, 1:2], rms[0:n, s, 1:2]).then_inc(dve_step, 1)
                dve.wait_ge(dve_step, at + 4)
                dve.wait_ge(h_turned, t * 2)
                nc.vector.scalar_tensor_tensor(h[0:n, s, :], x1[0:n, s, :], rstd[0:n, s, 1:2], gain_pre[0:n, :],
                                               ALU.mult, ALU.mult).then_inc(dve_step, 1)

            lo_mix(0, 0)
            for k in range(DBLK):
                dve.wait_ge(w_hi_ready, k + 1)
                nc.vector.tensor_tensor(w_lo[:, k, :], w[:, k % 2, :], f32(w_hi[:, k, :]), ALU.subtract).then_inc(w_lo_ready, 1)

            def step(t, s, k):
                if exists(t + 1):
                    lo_mix(t + 1, 1 - s)
                if exists(t - 1):
                    lo_h(t - 1, 1 - s)
                if exists(t):
                    rows(t, s, k)

            steps_of_tiles(dve, step)


def mlp(nc, d):
    GROUPS = 3
    GT = TOK // GROUPS
    GTILES = [(j * P, min(P, GT - j * P)) for j in range(-(-GT // P))]
    NT = len(GTILES)
    NG = GT // GRP
    CH = 2 * P
    CB = CH // P
    CHUNKS = FF // CH
    NUP = CB * NG
    ALL = GROUPS * CHUNKS
    assert CHUNKS // 2 == DEC_B and NUP == 4 and CHUNKS % 2 == 0 and SEQ % GT + GTILES[-1][1] == GT and GTILES[-1][1] == DEC

    with Phase(nc, "ml") as ph:
        eps = ph.sb("eps", [P, 1])
        gain = ph.sb("gain", [P, D])
        h_hi = ph.sb("h_hi", [P, DBLK, GT], F32R)
        h_lo = ph.sb("h_lo", [P, DBLK, GT], F32R)
        up = ph.sb("up", [P, 2, DBLK, CH])
        up_hi = ph.sb("up_hi", [P, 2, DBLK, CH], F32R)
        up_lo = ph.sb("up_lo", [P, 2, DBLK, CH], F32R)
        down = ph.sb("down", [P, 2, CB, D])
        down_hi = ph.sb("down_hi", [P, 2, CB, D], F32R)
        down_lo = ph.sb("down_lo", [P, 2, CB, D], F32R)
        r = ph.sb("r", [P, 2, GRP])
        a = ph.sb("a", [P, 2, GRP])
        a_hi = ph.sb("a_hi", [P, 2, CB, GT], F32R)
        a_lo = ph.sb("a_lo", [P, 2, CB, GT], F32R)
        y = ph.sb("y", [P, NT, D])
        x1 = ph.sb("x1", [P, 2, D])
        sumsq = ph.sb("sumsq", [P, 2])
        rms = ph.sb("rms", [P, 2])
        rstd = ph.sb("rstd", [P, 2])
        up_ps = ph.banks("up", NUP)
        down_ps = [ph.ctx.enter_context(nc.psum_tensor(f"ml_down{s}", [P, D], F32)) for s in range(2)]

        const_in = ph.sem("const_in")
        eps_ready = ph.sem("eps_ready")
        h_in = ph.sem("h_in")
        up_in = ph.sems("up_in", 2)
        down_in = ph.sems("down_in", 2)
        up_hi_ready = ph.sem("up_hi_ready")
        up_lo_ready = ph.sem("up_lo_ready")
        down_hi_ready = ph.sem("down_hi_ready")
        down_lo_ready = ph.sem("down_lo_ready")
        up_done = ph.sem("up_done")
        relu_done = ph.sem("relu_done")
        a_done = ph.sem("a_done")
        a_hi_done = ph.sem("a_hi_done")
        a_lo_done = ph.sem("a_lo_done")
        down_done = ph.sem("down_done")
        y_added = ph.sem("y_added")
        y_zero = ph.sem("y_zero")
        squared = ph.sem("squared")
        rms_ready = ph.sem("rms_ready")
        dve_step = ph.sem("dve_step")
        x1_in = ph.sems("x1_in", 2)
        y_out = ph.sem("y_out")
        cache_out = ph.sem("cache_out")

        up_v = d["w_up"].rearrange("l (k p) (f m) -> (l f) p k m", p=P, m=CH)
        down_v = d["w_down"].rearrange("l (f k p) c -> (l f) p k c", p=P, k=CB)

        block = ph.block()

        def chunk_steps(engine, g, step):
            n0 = g * CHUNKS
            with engine.Fori(0, CHUNKS // 2 - 1) as it:
                for s in range(2):
                    step(it * 2 + s, n0 + it * 2 + s, s, n0 // 2 + it, False)
            for c in range(CHUNKS - 2, CHUNKS):
                step(c, n0 + c, c % 2, n0 // 2 + c // 2, True)

        @block.sync
        def _(sp):
            sp.dma_start(gain[:], d["g_mlp_post"].partition_broadcast(P)).then_inc(const_in, 16)

            def load_up(c, n, s):
                if not isinstance(n, int) or n >= 2:
                    sp.wait_ge(up_lo_ready, n - 1)
                sp.dma_start(up[:, s, :, :], up_v[c]).then_inc(up_in[s], 16)

            def load_down(c, n, s):
                if not isinstance(n, int) or n >= 2:
                    sp.wait_ge(down_lo_ready, n - 1)
                sp.dma_start(down[:, s, :, :], down_v[c]).then_inc(down_in[s], 16)

            for g in range(GROUPS):
                if g:
                    sp.wait_ge(up_done, (2 + g * CHUNKS) * NUP)
                for part, frm in ((h_hi, d["h_hi"]), (h_lo, d["h_lo"])):
                    sp.dma_start(f32(part[:]), frm.rearrange("k p t -> p k t")[:, :, g * GT:(g + 1) * GT]).then_inc(h_in, 16)
                for s in range(2):
                    load_up(s, g * CHUNKS + s, s)
                    load_down(s, g * CHUNKS + s, s)
                with sp.Fori(1, CHUNKS // 2) as it:
                    for s in range(2):
                        load_up(it * 2 + s, g * CHUNKS + it * 2 + s, s)
                        load_down(it * 2 + s, g * CHUNKS + it * 2 + s, s)
                    if g < 2:
                        copy_cache(sp, *((d["cache_a_k"], d["o_a_k_s"]), (d["cache_a_v"], d["o_a_v_s"]))[g], it, 160, cache_out)
            copy_cache(sp, d["cache_a_k"], d["o_a_k_s"], 0, 160, cache_out)
            copy_cache(sp, d["cache_a_v"], d["o_a_v_s"], 0, 160, cache_out)
            sp.wait_ge(cache_out, 16 * DEC_B * 2)

        @block.gpsimd
        def _(pool):
            for j in range(NT):
                nc.gpsimd.memset(y[:, j, :], 0.0).then_inc(y_zero, 1)
            for g in range(GROUPS):
                for j, (t0, m) in enumerate(GTILES):
                    i = g * NT + j
                    pool.wait_ge(dve_step, 6 + i * 3 - 3)
                    rows = slice(g * GT + t0, g * GT + t0 + m)
                    pool.dma_start(x1[0:m, i % 2, :], d["x1"][rows, :]).then_inc(x1_in[i % 2], 16)
                    pool.wait_ge(dve_step, 6 + i * 3 + 3)
                    out = d["o_y_s"].rearrange("b t c -> (b t) c") if rows.start == SEQ else \
                        d["o_y_p"].rearrange("b t c -> (b t) c")[rows, :]
                    pool.dma_start(out, y[0:m, j, :]).then_inc(y_out, 16)
                if g < GROUPS - 1:
                    pool.wait_ge(y_out, 16 * NT * (g + 1))
                    for j in range(NT):
                        nc.gpsimd.memset(y[:, j, :], 0.0).then_inc(y_zero, 1)
            pool.wait_ge(y_out, 16 * NT * GROUPS)

        @block.tensor
        def _(pe):
            pe.sem_inc(up_done, 2 * NUP)
            pe.sem_inc(down_done, 2 * NT)

            def product_up(n, s):
                pe.wait_ge(up_lo_ready, n + 1)
                for b in range(CB):
                    for g in range(NG):
                        i = b * NG + g
                        pe.wait_ge(relu_done, n * NUP + i + 1)
                        out, cols, w = up_ps[i][:, 0:GRP], slice(g * GRP, (g + 1) * GRP), slice(b * P, (b + 1) * P)
                        for k in range(DBLK):
                            pe.matmul(out, up_hi[:, s, k, w], h_hi[:, k, cols], start=(k == 0), stop=False)
                            pe.matmul(out, up_hi[:, s, k, w], h_lo[:, k, cols], start=False, stop=False)
                            last = pe.matmul(out, up_lo[:, s, k, w], h_hi[:, k, cols], start=False, stop=(k == DBLK - 1))
                        last.then_inc(up_done, 1)

            def product_down(n, s):
                pe.wait_ge(down_lo_ready, n + 1)
                pe.wait_ge(a_lo_done, 2 + n * NUP + NUP)
                for j, (t0, m) in enumerate(GTILES):
                    pe.wait_ge(y_added, n * NT + j + 1)
                    for b in range(CB):
                        for p, w in ((a_hi, down_hi), (a_hi, down_lo), (a_lo, down_hi)):
                            for half in range(2):
                                cols = slice(half * 512, half * 512 + 512)
                                last = pe.matmul(down_ps[j % 2][0:m, cols], p[:, s, b, t0:t0 + m], w[:, s, b, cols],
                                                 start=(b == 0 and p is a_hi and w is down_hi),
                                                 stop=(b == CB - 1 and p is a_lo))
                    last.then_inc(down_done, 1)

            for g in range(GROUPS):
                pe.wait_ge(h_in, 32 * (g + 1))
                product_up(g * CHUNKS, 0)

                def step(c, n, s, k, tail):
                    if not (tail and c == CHUNKS - 1):
                        product_up(n + 1, 1 - s)
                    product_down(n, s)

                chunk_steps(pe, g, step)

        @block.scalar
        def _(act):
            act.sem_inc(relu_done, NUP)

            def split_up(n, s, k):
                act.wait_ge(up_in[s], k * 16 + 16)
                act.wait_ge(up_done, (n + 1) * NUP)
                nc.scalar.copy(up_hi[:, s, :, :], up[:, s, :, :]).then_inc(up_hi_ready, 1)

            def split_down(n, s, k):
                act.wait_ge(down_in[s], k * 16 + 16)
                act.wait_ge(down_done, (n + 1) * NT)
                nc.scalar.copy(down_hi[:, s, :, :], down[:, s, :, :]).then_inc(down_hi_ready, 1)

            def hidden(n, s):
                def relu(i):
                    act.wait_ge(up_done, (n + 2) * NUP + i + 1)
                    act.wait_ge(a_done, n * NUP + i + 1)
                    nc.scalar.activation(r[:, i % 2, :], up_ps[i][:, 0:GRP], ACT.Relu).then_inc(relu_done, 1)

                def high(i):
                    b, g = divmod(i, NG)
                    act.wait_ge(a_done, 2 + n * NUP + i + 1)
                    act.wait_ge(down_done, (n + 1) * NT)
                    nc.scalar.copy(a_hi[:, s, b, g * GRP:(g + 1) * GRP], a[:, i % 2, :]).then_inc(a_hi_done, 1)

                relu(0)
                for i in range(NUP):
                    if i + 1 < NUP:
                        relu(i + 1)
                    high(i)

            split_up(0, 0, 0)
            split_up(1, 1, 0)
            split_down(0, 0, 0)
            act.wait_ge(eps_ready, 1)
            for g in range(GROUPS):
                hidden(g * CHUNKS, 0)

                def step(c, n, s, k, tail):
                    if not tail or n + 1 < ALL:
                        split_down(n + 1, 1 - s, k + s)
                    if not tail or n + 2 < ALL:
                        split_up(n + 2, s, k + 1)
                    if not (tail and c == CHUNKS - 1):
                        hidden(n + 1, 1 - s)

                chunk_steps(act, g, step)
                act.wait_ge(y_added, 2 + (g + 1) * CHUNKS * NT)
                for j, (t0, m) in enumerate(GTILES):
                    i = g * NT + j
                    s = i % 2
                    act.wait_ge(dve_step, 6 + i * 3 - 5)
                    act.wait_ge(squared, i)
                    nc.scalar.activation(down_ps[s][0:m, :], y[0:m, j, :], ACT.Square, scale=D ** -0.5,
                                         accum_out=sumsq[0:m, s:s + 1]).then_inc(squared, 1)
                    act.wait_ge(squared, i + 1)
                    nc.scalar.activation(rms[0:m, s:s + 1], sumsq[0:m, s:s + 1], ACT.Sqrt,
                                         bias=eps[0:m, :]).then_inc(rms_ready, 1)

        @block.vector
        def _(dve):
            nc.vector.memset(eps[:], EPS).then_inc(eps_ready, 1)
            dve.sem_inc(a_done, 2)
            dve.sem_inc(a_lo_done, 2)
            dve.sem_inc(y_added, 2)
            dve.sem_inc(dve_step, 6)
            dve.wait_ge(const_in, 16)

            def split_up(n, s):
                dve.wait_ge(up_hi_ready, n + 1)
                nc.vector.tensor_tensor(up_lo[:, s, :, :], up[:, s, :, :], f32(up_hi[:, s, :, :]),
                                        ALU.subtract).then_inc(up_lo_ready, 1)

            def split_down(n, s):
                dve.wait_ge(down_hi_ready, n + 1)
                nc.vector.tensor_tensor(down_lo[:, s, :, :], down[:, s, :, :], f32(down_hi[:, s, :, :]),
                                        ALU.subtract).then_inc(down_lo_ready, 1)

            def hidden(n, s):
                def square(i):
                    dve.wait_ge(relu_done, (n + 1) * NUP + i + 1)
                    dve.wait_ge(a_lo_done, n * NUP + i + 1)
                    nc.vector.tensor_tensor(a[:, i % 2, :], r[:, i % 2, :], r[:, i % 2, :], ALU.mult).then_inc(a_done, 1)

                def low(i):
                    b, g = divmod(i, NG)
                    at = (slice(None), s, b, slice(g * GRP, (g + 1) * GRP))
                    dve.wait_ge(a_hi_done, n * NUP + i + 1)
                    nc.vector.tensor_tensor(a_lo[at], a[:, i % 2, :], f32(a_hi[at]), ALU.subtract).then_inc(a_lo_done, 1)

                square(0)
                for i in range(NUP):
                    if i + 1 < NUP:
                        square(i + 1)
                    low(i)

            def add_y(n):
                for j, (t0, m) in enumerate(GTILES):
                    dve.wait_ge(down_done, (n + 2) * NT + j + 1)
                    nc.vector.tensor_tensor(y[0:m, j, :], down_ps[j % 2][0:m, :], y[0:m, j, :], ALU.add).then_inc(y_added, 1)

            split_up(0, 0)
            split_up(1, 1)
            split_down(0, 0)
            for g in range(GROUPS):
                hidden(g * CHUNKS, 0)
                dve.wait_ge(y_zero, NT * (g + 1))

                def step(c, n, s, k, tail):
                    if not tail or n + 1 < ALL:
                        split_down(n + 1, 1 - s)
                    if not tail or n + 2 < ALL:
                        split_up(n + 2, s)
                    if not (tail and c == CHUNKS - 1):
                        hidden(n + 1, 1 - s)
                    dve.wait_ge(y_added, 2 + n * NT)
                    add_y(n)

                chunk_steps(dve, g, step)
                for j, (t0, m) in enumerate(GTILES):
                    i = g * NT + j
                    s = i % 2
                    dve.wait_ge(rms_ready, i + 1)
                    nc.vector.reciprocal(rstd[0:m, s:s + 1], rms[0:m, s:s + 1]).then_inc(dve_step, 1)
                    dve.wait_ge(dve_step, 6 + i * 3 + 1)
                    nc.vector.scalar_tensor_tensor(y[0:m, j, :], y[0:m, j, :], rstd[0:m, s:s + 1], gain[0:m, :],
                                                   ALU.mult, ALU.mult).then_inc(dve_step, 1)
                    dve.wait_ge(dve_step, 6 + i * 3 + 2)
                    dve.wait_ge(x1_in[s], 16 * (i // 2 + 1))
                    nc.vector.tensor_tensor(y[0:m, j, :], y[0:m, j, :], x1[0:m, s, :], ALU.add).then_inc(dve_step, 1)


def decode(nc, d):
    NEAR = 512
    FAR_T = (PAST - NEAR) // (2 * P)
    NEAR_T = NEAR // P
    KT = FAR_T + NEAR_T
    A_KEYS = KT * P + DEC_T
    B_KEYS = BWIN + DEC_T
    QH = DEC_T * AH
    QUADS = [range(0, 4), range(4, 8), range(8, KT + 1)]
    NX = 3 * len(QUADS) + 1
    assert AH == BH and DEC_T * 2 == 16

    with Phase(nc, "de") as ph:
        ident = ph.sb("ident", [P, P])
        qa_raw = ph.sb("qa_raw", [P, 3, DEC])
        qb_raw = ph.sb("qb_raw", [P, 3, DEC])
        qa = ph.sb("qa", [P, 3, DEC_B, DEC_T, AH])
        qb = ph.sb("qb", [P, DEC_B, DEC_T, BH])
        q_now = ph.sb("q_now", [P, 2, 4, QH])
        bias_rows = ph.sb("bias_rows", [QH, PAST + DEC_T])
        bias = ph.sb("bias", [QH, A_KEYS + B_KEYS])
        own = ph.sb("own", [QH, AH, HD])
        pick = ph.sb("pick", [P, DEC_T])
        k = ph.sb("k", [P, 2, KT, AW])
        v = ph.sb("v", [P, 2, KT, AW])
        kb = ph.sb("kb", [P, 2, KVW])
        vb = ph.sb("vb", [P, 2, KVW])
        new = ph.sb("new", [P, 2, D])
        k_t = ph.sb("k_t", [P, 3, 512])
        prob = ph.sb("prob", [QH, 2, A_KEYS + B_KEYS])
        top = ph.sb("top", [QH, 2, 4])
        minus_max = ph.sb("minus_max", [QH, 2, 2])
        total = ph.sb("total", [QH, 2, 2])
        sink = ph.sb("sink", [QH, 1])
        sink_exp = ph.sb("sink_exp", [QH, 2])
        inverse = ph.sb("inverse", [QH, 2, 2])
        p_t = ph.sb("p_t", [P, KT + 3, QH])
        o = ph.sb("o", [P, 2, AH * HD])
        rows = ph.sb("rows", [DEC_T, 2, AW + BW])
        kt_ps = ph.banks("kt", 2)
        s_ps = ph.banks("s", 2)
        pt_ps = ph.banks("pt", 1)[0]
        o_ps = ph.banks("o", 1)[0]
        row_ps = ph.banks("row", 2)

        const_in = ph.sem("const_in")
        zeroed = ph.sem("zeroed")
        prepared = ph.sem("prepared")
        q_ready = ph.sem("q_ready")
        k_in = ph.sems("k_in", 2)
        v_in = ph.sems("v_in", 2)
        kt_ready = ph.sem("kt_ready")
        kt_copied = ph.sem("kt_copied")
        scored = ph.sem("scored")
        biased = ph.sem("biased")
        max_ready = ph.sem("max_ready")
        exped = ph.sem("exped")
        sink_ready = ph.sem("sink_ready")
        summed = ph.sem("summed")
        inverted = ph.sem("inverted")
        pt_ready = ph.sem("pt_ready")
        pt_copied = ph.sem("pt_copied")
        weighed = ph.sem("weighed")
        o_ready = ph.sem("o_ready")
        picked = ph.sem("picked")
        rows_ready = ph.sem("rows_ready")
        rows_out = ph.sems("rows_out", 2)

        PT_GROUPS = [range(0, 5), range(5, 10), range(10, KT + 3)]
        pt_cols = d["pt"].rearrange("f p t -> p f t")

        def tile_cols(t):
            if t < KT:
                return slice(t * P, (t + 1) * P)
            a, n = {KT: (KT * P, DEC_T), KT + 1: (A_KEYS, P), KT + 2: (A_KEYS + BWIN, DEC_T)}[t]
            return slice(a, a + n)

        block = ph.block()

        def steps(engine, step):
            with engine.Fori(0, DEC_B // 2 - 1) as it:
                for s in range(2):
                    step(it * 2 + s, s, it, False)
            for b in range(DEC_B - 2, DEC_B):
                step(b, b % 2, b // 2, b == DEC_B - 1)

        @block.sync
        def _(sp):
            sp.dma_start(ident[:], d["c_ident"]).then_inc(const_in, 16)
            sp.dma_start(own[:], d["c_own"]).then_inc(const_in, 16)
            sp.dma_start(pick[:], d["c_pick"]).then_inc(const_in, 16)
            sp.dma_start(qa_raw[:], pt_cols[:, AQ0:AQ0 + 3, SEQ:]).then_inc(const_in, 16)
            sp.dma_start(qb_raw[:], pt_cols[:, BQ0:BQ0 + 3, SEQ:]).then_inc(const_in, 16)
            for q in range(DEC_T):
                src = bass.AP(d["source"].tensor, DEC_T - 1 - q, [[GR, AH], [1, PAST + DEC_T]])
                sp.dma_start(bias_rows[q * AH:(q + 1) * AH, :], src).then_inc(const_in, 16)
                src = bass.AP(d["source"].tensor, AH * GR + PAST + DEC_T - 1 - BWIN - q, [[GR, BH], [1, B_KEYS]])
                sp.dma_start(bias[q * AH:(q + 1) * AH, A_KEYS:], src).then_inc(const_in, 16)
                sp.dma_start(sink[q * AH:(q + 1) * AH, :], d["b_sinks"].rearrange("l h -> h l")).then_inc(const_in, 16)
            sp.wait_ge(zeroed, 4)

            def load(b, s, first):
                if not first:
                    sp.wait_ge(scored, (b + 1) * NX)
                for which, (big, cache, small, cache_b, sem) in enumerate((
                        (k, d["cache_a_k"], kb, d["cache_b_k"], k_in), (v, d["cache_a_v"], vb, d["cache_b_v"], v_in))):
                    if which and not first:
                        sp.wait_ge(weighed, 4 + (b - 1) * 2)
                    flat = cache.rearrange("l b t h e -> (l b) t (h e)")[b]
                    for t in range(FAR_T):
                        far = flat[t * 2 * P:(t + 1) * 2 * P, :].rearrange("(g r) c -> g r c", r=16)[:, 0:DEC_T, :]
                        sp.dma_start(big[:, s, t, :], far).then_inc(sem[s], 16)
                    sp.dma_start(big[:, s, FAR_T:, :],
                                 flat[PAST - NEAR:, :].rearrange("(t p) c -> p t c", p=P)).then_inc(sem[s], 16)
                    sp.dma_start(small[:, s, :], cache_b.rearrange("l b t h e -> (l b) t (h e)")[b]).then_inc(sem[s], 16)
                    if not which:
                        if not first:
                            sp.wait_ge(weighed, 4 + (b - 1) * 2)
                        sp.dma_start(new[0:DEC_T, s, :],
                                     d["kv"][SEQ:, :].rearrange("(b t) c -> b t c", t=DEC_T)[b]).then_inc(k_in[s], 16)

            load(0, 0, True)
            load(1, 1, True)
            with sp.Fori(1, DEC_B // 2) as it:
                for s in range(2):
                    load(it * 2 + s, s, False)

        @block.gpsimd
        def _(pool):
            nc.gpsimd.memset(qa[:], 0.0).then_inc(zeroed, 1)
            nc.gpsimd.memset(qb[:], 0.0).then_inc(zeroed, 1)
            nc.gpsimd.memset(new[:], 0.0).then_inc(zeroed, 1)
            nc.gpsimd.memset(p_t[:], 0.0).then_inc(zeroed, 1)
            nc.gpsimd.memset(o[:], 0.0).then_inc(zeroed, 1)

        @block.tensor
        def _(pe):
            pe.sem_inc(scored, 2 * NX)
            pe.sem_inc(weighed, 4)
            pe.sem_inc(picked, 1)
            pe.wait_ge(const_in, 16 * (5 + 3 * DEC_T))
            pe.wait_ge(zeroed, 5)

            def turn_keys(b, s, x):
                pe.wait_ge(kt_copied, b * NX + x + 1)
                out = kt_ps[x % 2]
                if x == NX - 1:
                    pe.transpose(out[:, 0:P], kb[:, s, :], ident[:])
                    last = pe.transpose(out[:, P:P + DEC_T], new[0:DEC_T, s, 2 * AW:2 * AW + KVW], ident[0:DEC_T, 0:DEC_T])
                else:
                    quad, pair = QUADS[x // 3], x % 3
                    for j, t in enumerate(quad):
                        if t < KT:
                            last = pe.transpose(out[:, j * P:(j + 1) * P], k[:, s, t, pair * P:(pair + 1) * P], ident[:])
                        else:
                            last = pe.transpose(out[:, j * P:j * P + DEC_T], new[0:DEC_T, s, pair * P:(pair + 1) * P],
                                                ident[0:DEC_T, 0:DEC_T])
                last.then_inc(kt_ready, 1)

            def score(b, s, x):
                pe.wait_ge(kt_copied, 2 + b * NX + x + 1)
                if x % 3 == 0:
                    pe.wait_ge(biased, b * 4 + x // 3 + 2 + 1)
                if x == NX - 1:
                    out, n = s_ps[1][0:QH, 0:B_KEYS], B_KEYS
                    pe.matmul(out, q_now[:, s, 3, :], k_t[:, x % 3, 0:n], start=True, stop=True).then_inc(scored, 1)
                else:
                    n = min(512, A_KEYS - (x // 3) * 512)
                    pe.matmul(s_ps[x // 3 % 2][0:QH, 0:n], q_now[:, s, x % 3, :], k_t[:, x % 3, 0:n], start=(x % 3 == 0),
                              stop=(x % 3 == 2)).then_inc(scored, 1)

            def scores(b, s, visit):
                pe.wait_ge(k_in[s], (visit + 1) * 16 * (FAR_T + 3))
                pe.wait_ge(q_ready, b + 1)
                for x in range(NX + 1):
                    if x < NX:
                        turn_keys(b, s, x)
                    if x:
                        score(b, s, x - 1)

            def turn_probs(b, s, g):
                pe.wait_ge(exped, b * 2 + (1 if g < 2 else 2))
                pe.wait_ge(pt_copied, b * 3 + g + 3)
                apart(pe)
                for j, t in enumerate(PT_GROUPS[g]):
                    c = tile_cols(t)
                    last = pe.transpose(pt_ps[0:c.stop - c.start, j * QH:(j + 1) * QH], prob[:, s, c], ident[0:QH, 0:QH])
                last.then_inc(pt_ready, 1)

            def weigh(b, s, visit):
                for g in range(3):
                    turn_probs(b, s, g)
                pe.wait_ge(v_in[s], (visit + 1) * 16 * (FAR_T + 2))
                pe.wait_ge(o_ready, 3 + b * 3)
                pe.wait_ge(pt_copied, 3 + b * 3 + 3)
                for t in range(KT + 1):
                    rhs = v[:, s, t, :] if t < KT else new[:, s, AW:2 * AW]
                    last = pe.matmul(o_ps[0:QH, 0:AW], p_t[:, t, :], rhs, start=(t == 0), stop=(t == KT))
                last.then_inc(weighed, 1)
                pe.wait_ge(o_ready, 3 + b * 3 + 1)
                pe.matmul(o_ps[0:QH, 0:KVW], p_t[:, KT + 1, :], vb[:, s, :], start=True, stop=False)
                pe.matmul(o_ps[0:QH, 0:KVW], p_t[:, KT + 2, :], new[:, s, 2 * AW + KVW:], start=False,
                          stop=True).then_inc(weighed, 1)
                pe.wait_ge(o_ready, 3 + b * 3 + 3)
                pe.wait_ge(rows_ready, b + 1)
                for i in range(2):
                    last = pe.matmul(row_ps[i][0:DEC_T, 0:AW], pick[:], o[:, i, :], start=True, stop=True)
                last.then_inc(picked, 1)

            scores(0, 0, 0)

            def step(b, s, visit, last):
                if not last:
                    scores(b + 1, 1 - s, visit + s)
                weigh(b, s, visit)

            steps(pe, step)

        @block.scalar
        def _(act):
            act.sem_inc(kt_copied, 2)
            act.sem_inc(rows_ready, 1)
            for s in range(2):
                act.sem_inc(rows_out[s], 16)

            def copy_keys(b, s):
                for x in range(NX):
                    n = B_KEYS if x == NX - 1 else min(512, A_KEYS - (x // 3) * 512)
                    act.wait_ge(kt_ready, b * NX + x + 1)
                    act.wait_ge(scored, 2 * NX + b * NX + x - 2)
                    nc.scalar.copy(k_t[:, x % 3, 0:n], kt_ps[x % 2][:, 0:n]).then_inc(kt_copied, 1)

            def exp(b, s):
                for i, (c0, c1) in enumerate(((0, A_KEYS), (A_KEYS, A_KEYS + B_KEYS))):
                    act.wait_ge(max_ready, b * 2 + i + 1)
                    if i:
                        nc.scalar.activation(sink_exp[:, s:s + 1], sink[:, 0:1], ACT.Exp,
                                             bias=minus_max[:, s, 1:2]).then_inc(sink_ready, 1)
                    nc.scalar.activation(prob[:, s, c0:c1], prob[:, s, c0:c1], ACT.Exp, bias=minus_max[:, s, i:i + 1],
                                         accum_out=total[:, s, i:i + 1]).then_inc(exped, 1)

            def copy_rows(b, s, visit):
                act.wait_ge(picked, 1 + b + 1)
                act.wait_ge(rows_out[s], visit * 16 + 16)
                nc.scalar.copy(rows[:, s, 0:AW], row_ps[0][0:DEC_T, 0:AW])
                nc.scalar.copy(rows[:, s, AW:], row_ps[1][0:DEC_T, 0:BW]).then_inc(rows_ready, 1)
                act.wait_ge(rows_ready, 1 + b + 1)
                act.dma_start(d["mix"][SEQ:, :].rearrange("(b t) c -> b t c", t=DEC_T)[b], rows[:, s, :]).then_inc(rows_out[s], 16)

            copy_keys(0, 0)
            exp(0, 0)

            def step(b, s, visit, last):
                if not last:
                    copy_keys(b + 1, 1 - s)
                    exp(b + 1, 1 - s)
                copy_rows(b, s, visit)

            steps(act, step)
            for s in range(2):
                act.wait_ge(rows_out[s], 16 + 16 * (DEC_B // 2))

        @block.vector
        def _(dve):
            dve.sem_inc(biased, 4)
            dve.sem_inc(pt_copied, 3)
            dve.sem_inc(o_ready, 3)
            dve.wait_ge(const_in, 16 * (5 + 3 * DEC_T))
            dve.wait_ge(zeroed, 5)
            n = 0
            for h in range(AH):
                half = slice((h % 2) * HD, (h % 2) * HD + HD)
                key = slice((h // 3) * HD, (h // 3) * HD + HD)
                bt = lambda ap: ap.rearrange("p (b t) -> p b t", b=DEC_B)
                nc.vector.tensor_scalar(qa[half, h // 2, :, :, h], bt(qa_raw[half, h // 2, :]), 1.0, None,
                                        ALU.mult).then_inc(prepared, 1)
                nc.vector.tensor_scalar(qb[key, :, :, h], bt(qb_raw[half, h // 2, :]), 1.0, None,
                                        ALU.mult).then_inc(prepared, 1)
                n += 2
            far = bias_rows[:, 0:PAST - NEAR].rearrange("p (g r) -> p g r", r=16)[:, :, 0:DEC_T]
            nc.vector.tensor_copy(bias[:, 0:FAR_T * P].rearrange("p (g r) -> p g r", r=DEC_T), far).then_inc(prepared, 1)
            nc.vector.tensor_copy(bias[:, FAR_T * P:A_KEYS], bias_rows[:, PAST - NEAR:]).then_inc(prepared, 1)
            dve.wait_ge(prepared, n + 2)

            def queries(b, s):
                dve.wait_ge(scored, (b + 1) * NX)
                nc.vector.tensor_copy(q_now[:, s, 0:3, :], qa[:, :, bass.ds(b, 1), :, :].rearrange(
                    "p j b t h -> p j (b t h)"))
                nc.vector.tensor_copy(q_now[:, s, 3, :], qb[:, bass.ds(b, 1), :, :].rearrange(
                    "p b t h -> p (b t h)")).then_inc(q_ready, 1)

            def add_bias(b, s):
                for c in range(4):
                    c0, n = (A_KEYS, B_KEYS) if c == 3 else (c * 512, min(512, A_KEYS - c * 512))
                    dve.wait_ge(scored, 2 * NX + b * NX + (NX if c == 3 else 3 * c + 3))
                    apart(dve)
                    nc.vector.tensor_tensor_reduce(prob[:, s, c0:c0 + n], s_ps[c % 2][0:QH, 0:n], bias[:, c0:c0 + n], 1.0,
                                                   sink[:, 0:1] if c == 3 else MASKED, ALU.add, ALU.max,
                                                   top[:, s, c:c + 1]).then_inc(biased, 1)
                for i, (c0, c1) in enumerate(((0, 3), (3, 4))):
                    dve.wait_ge(biased, 4 + b * 4 + c1)
                    nc.vector.tensor_reduce(minus_max[:, s, i:i + 1], top[:, s, c0:c1], AX, ALU.max,
                                            negate=True).then_inc(max_ready, 1)

            def copy_probs(b, s):
                for g, tiles in enumerate(PT_GROUPS):
                    dve.wait_ge(pt_ready, b * 3 + g + 1)
                    dve.wait_ge(weighed, 4 + b * 2)
                    if g < 2:
                        last = nc.vector.tensor_copy(p_t[:, tiles[0]:tiles[-1] + 1, :], pt_ps[:, 0:len(tiles) * QH].rearrange(
                            "p (t q) -> p t q", q=QH))
                    else:
                        for j, t in enumerate(tiles):
                            c = tile_cols(t)
                            last = nc.vector.tensor_copy(p_t[0:c.stop - c.start, t, :],
                                                         pt_ps[0:c.stop - c.start, j * QH:(j + 1) * QH])
                    last.then_inc(pt_copied, 1)

            def normalise(b, s):
                dve.wait_ge(sink_ready, b + 1)
                nc.vector.tensor_tensor(total[:, s, 1:2], total[:, s, 1:2], sink_exp[:, s:s + 1], ALU.add).then_inc(summed, 1)
                dve.wait_ge(summed, b + 1)
                nc.vector.reciprocal(inverse[:, s, :], total[:, s, :]).then_inc(inverted, 1)
                dve.wait_ge(inverted, b + 1)
                dve.wait_ge(picked, 1 + b)
                dve.wait_ge(weighed, 4 + b * 2 + 1)
                heads = o[0:QH, :, :].rearrange("p i (h e) -> p i h e", h=AH)
                nc.vector.scalar_tensor_tensor(o[0:QH, 0, :], o_ps[0:QH, 0:AW], inverse[:, s, 0:1],
                                               own[:].rearrange("p h e -> p (h e)"), ALU.mult, ALU.mult).then_inc(o_ready, 1)
                dve.wait_ge(weighed, 4 + b * 2 + 2)
                for kv in range(KVH):
                    src = o_ps[0:QH, kv * HD:(kv + 1) * HD].unsqueeze(1).to_broadcast([QH, 3, HD])
                    nc.vector.scalar_tensor_tensor(heads[:, 1, 3 * kv:3 * kv + 3, :], src, inverse[:, s, 1:2],
                                                   own[:, 3 * kv:3 * kv + 3, :], ALU.mult, ALU.mult).then_inc(o_ready, 1)

            queries(0, 0)
            add_bias(0, 0)

            def step(b, s, visit, last):
                if not last:
                    queries(b + 1, 1 - s)
                    add_bias(b + 1, 1 - s)
                copy_probs(b, s)
                normalise(b, s)

            steps(dve, step)


def constants():
    row = np.arange(P)
    fold = np.zeros((P, P), np.float32)
    fold[row, row % HD] = 1.0
    scores = np.arange(DEC_T * AH)
    own = np.zeros((DEC_T * AH, AH, HD), np.float32)
    own[scores, scores % AH] = 1.0
    pick = np.zeros((P, DEC_T), np.float32)
    pick[scores, scores // AH] = 1.0
    scale = np.ones((P, FBLK), np.float32)
    scale[:, AQ0:AK0] = scale[:, BQ0:BK0] = SCALE
    return {"c_ident": np.eye(P, dtype=np.float32), "c_scale": scale, "c_fold": fold, "c_own": own, "c_pick": pick,
            "c_bucket_a": bucket_rows(a_counts), "c_bucket_b": bucket_rows(b_counts)}


SCRATCH = {
    "pt": (FBLK, P, TOK),
    "kv": (TOK, D),
    "oct": (2, P, TOK),
    "source": (2, AH, GR),
    "spread": (2, AH, P, GR),
    "mix": (TOK, AW + BW),
    "x1": (TOK, D),
    "h_hi": (DBLK, P, TOK),
    "h_lo": (DBLK, P, TOK),
}


def build(nc, tensors):
    scratch = {name: nc.dram_tensor(f"scratch_{name}", shape, F32).ap() for name, shape in SCRATCH.items()}
    d = {**tensors, **scratch}
    project(nc, d)
    rows_and_tables(nc, d)
    attend(nc, d, "a")
    attend(nc, d, "b")
    decode(nc, d)
    out_project(nc, d)
    mlp(nc, d)


_INS = ["x_prompt", "x_sample", "cache_a_k", "cache_a_v", "cache_b_k", "cache_b_v", "state_conv", "w_in", "w_out",
        "conv_w", "rel_bias", "b_sinks", "g_mix_pre", "g_mix_post", "w_up", "w_down", "g_mlp_pre", "g_mlp_post"]
_OUTS = [("o_y_p", (1, SEQ, D)), ("o_y_s", (DEC_B, DEC_T, D)),
         ("o_a_k_p", (1, 1, SEQ, AH, HD)), ("o_a_v_p", (1, 1, SEQ, AH, HD)),
         ("o_b_k_p", (1, 1, BWIN, KVH, HD)), ("o_b_v_p", (1, 1, BWIN, KVH, HD)), ("o_conv_p", (1, 1, 2, CW)),
         ("o_a_k_s", (1, DEC_B, PAST, AH, HD)), ("o_a_v_s", (1, DEC_B, PAST, AH, HD)),
         ("o_b_k_s", (1, DEC_B, BWIN, KVH, HD)), ("o_b_v_s", (1, DEC_B, BWIN, KVH, HD)),
         ("o_conv_s", (1, DEC_B, 2, CW))]


def kernel(**inputs):
    import concourse.bacc as bacc
    from concourse.bass_utils import run_bass_kernel_spmd

    nc = bacc.Bacc("TRN2", target_bir_lowering=False, num_devices=1)
    tensors, arrays = {}, {}
    given = {name: np.ascontiguousarray(inputs[name]) for name in _INS}
    for name, a in {**given, **constants()}.items():
        arrays[f"in_{name}"] = a
        tensors[name] = nc.dram_tensor(f"in_{name}", a.shape, mybir.dt.from_np(a.dtype), kind="ExternalInput").ap()
    for name, shape in _OUTS:
        tensors[name] = nc.dram_tensor(f"out_{name}", shape, F32, kind="ExternalOutput").ap()
    build(nc, tensors)
    r = run_bass_kernel_spmd(nc, [arrays], core_ids=[0])
    return tuple(r.results[0][f"out_{name}"] for name, _ in _OUTS)
```
